# Optimizing a Trainium2 kernel written in Bass

```python
import math
import jax, jax.numpy as jnp
from jax import lax
import numpy as np

D_MODEL = 2048
BATCH = 1
SEQ = 256
DEPTH = 1

CHUNK = 64
HEAD_DIM = 128
EPS = 1e-6
A_HEADS = D_MODEL // HEAD_DIM
A_LEFT_CHUNKS = 8
A_BAND = (A_LEFT_CHUNKS + 1) * CHUNK
A_MAX_REL = 128
A_WIDTH = A_HEADS * HEAD_DIM
B_HEADS = D_MODEL // (2 * HEAD_DIM)
B_QK_WIDTH = B_HEADS * 2 * HEAD_DIM
B_V_WIDTH = B_HEADS * 2 * HEAD_DIM
Q_BLOCK = 128
C_WIDTH = D_MODEL
C_GROUPS = 16
CONV_K = 3
N_BRANCH = 3
D_FF = 4 * D_MODEL
IN_COLS = 3 * A_WIDTH + 2 * B_QK_WIDTH + B_V_WIDTH + 3 * C_WIDTH

kernel_name = "chunk_causal_hybrid_gated_trunk"

def _rms(x, g):
    xf = x.astype(jnp.float32)
    y = xf * lax.rsqrt(jnp.mean(xf * xf, axis=-1, keepdims=True) + EPS)
    return (y * g.astype(jnp.float32)).astype(x.dtype)

def _chunked_relpos_attention(q, k, v, rel_bias):
    B, S, H, d = q.shape
    n_chunks = S // CHUNK
    pad = A_LEFT_CHUNKS * CHUNK
    kp = jnp.pad(k, ((0, 0), (pad, 0), (0, 0), (0, 0)))
    vp = jnp.pad(v, ((0, 0), (pad, 0), (0, 0), (0, 0)))
    qc = q.reshape(B, n_chunks, CHUNK, H, d)
    i_idx = jnp.arange(CHUNK)[:, None]
    j_idx = jnp.arange(A_BAND)
    rel = jnp.clip(i_idx + pad - j_idx[None, :], -A_MAX_REL, A_MAX_REL) + A_MAX_REL
    bias = rel_bias[:, rel].astype(jnp.float32)
    scale = d ** -0.5

    def one_chunk(c):
        q_c = lax.dynamic_index_in_dim(qc, c, axis=1, keepdims=False)
        k_b = lax.dynamic_slice_in_dim(kp, c * CHUNK, A_BAND, axis=1)
        v_b = lax.dynamic_slice_in_dim(vp, c * CHUNK, A_BAND, axis=1)
        s = jnp.einsum('bqhd,bkhd->bhqk', q_c, k_b,
                       preferred_element_type=jnp.float32) * scale + bias[None]
        valid = j_idx >= pad - c * CHUNK
        s = jnp.where(valid[None, None, None, :], s, -jnp.inf)
        p = jax.nn.softmax(s, axis=-1).astype(v.dtype)
        return jnp.einsum('bhqk,bkhd->bqhd', p, v_b)

    out = lax.map(one_chunk, jnp.arange(n_chunks))
    return out.transpose(1, 0, 2, 3, 4).reshape(B, S, H * d)

def _differential_attention(q1, q2, k1, k2, v, lam):
    B, S, H, d = q1.shape
    n_blocks = S // Q_BLOCK
    key_chunk = jnp.arange(S) // CHUNK
    scale = d ** -0.5
    q1b = q1.reshape(B, n_blocks, Q_BLOCK, H, d)
    q2b = q2.reshape(B, n_blocks, Q_BLOCK, H, d)

    def one_block(n):
        a1 = lax.dynamic_index_in_dim(q1b, n, axis=1, keepdims=False)
        a2 = lax.dynamic_index_in_dim(q2b, n, axis=1, keepdims=False)
        q_chunk = (n * Q_BLOCK + jnp.arange(Q_BLOCK)) // CHUNK
        mask = (key_chunk[None, :] <= q_chunk[:, None])[None, None]
        s1 = jnp.einsum('bqhd,bkhd->bhqk', a1, k1, preferred_element_type=jnp.float32) * scale
        s2 = jnp.einsum('bqhd,bkhd->bhqk', a2, k2, preferred_element_type=jnp.float32) * scale
        p1 = jax.nn.softmax(jnp.where(mask, s1, -jnp.inf), axis=-1)
        p2 = jax.nn.softmax(jnp.where(mask, s2, -jnp.inf), axis=-1)
        p = (p1 - lam * p2).astype(v.dtype)
        return jnp.einsum('bhqk,bkhe->bqhe', p, v)

    out = lax.map(one_block, jnp.arange(n_blocks))
    return out.transpose(1, 0, 2, 3, 4).reshape(B, S, H, 2 * d)

def _short_gated_conv(bg, cg, xin, conv_w):
    u = cg * xin
    y = lax.conv_general_dilated(u, conv_w[:, None, :].astype(u.dtype), window_strides=(1,),
                                 padding=[(CONV_K - 1, 0)],
                                 dimension_numbers=('NWC', 'WIO', 'NWC'),
                                 feature_group_count=C_WIDTH)
    return bg * y

def setup_inputs(seed: int = 0) -> dict:
    key = jax.random.key(seed)
    ks = jax.random.split(key, 24)
    f32 = jnp.float32

    def nrm(k, shape, scale):
        return jax.random.normal(k, shape, f32) * scale

    D = D_MODEL
    return {
        "x": nrm(ks[0], (BATCH, SEQ, D), 1.0),
        "norm1_g": 1.0 + nrm(ks[1], (DEPTH, D), 0.02),
        "w_in": nrm(ks[2], (DEPTH, D, IN_COLS), D ** -0.5),
        "w_gate": nrm(ks[3], (DEPTH, D, N_BRANCH * D), D ** -0.5),
        "b_gate": nrm(ks[4], (DEPTH, N_BRANCH * D), 0.01),
        "a_qn_g": 1.0 + nrm(ks[5], (DEPTH, HEAD_DIM), 0.02),
        "a_kn_g": 1.0 + nrm(ks[6], (DEPTH, HEAD_DIM), 0.02),
        "a_rel_bias": nrm(ks[7], (DEPTH, A_HEADS, 2 * A_MAX_REL + 1), 0.1),
        "b_qn_g": 1.0 + nrm(ks[8], (DEPTH, HEAD_DIM), 0.02),
        "b_kn_g": 1.0 + nrm(ks[9], (DEPTH, HEAD_DIM), 0.02),
        "b_lq1": nrm(ks[10], (DEPTH, HEAD_DIM), 0.1),
        "b_lk1": nrm(ks[11], (DEPTH, HEAD_DIM), 0.1),
        "b_lq2": nrm(ks[12], (DEPTH, HEAD_DIM), 0.1),
        "b_lk2": nrm(ks[13], (DEPTH, HEAD_DIM), 0.1),
        "b_subln_g": 1.0 + nrm(ks[14], (DEPTH, 2 * HEAD_DIM), 0.02),
        "c_conv_w": nrm(ks[15], (DEPTH, CONV_K, C_WIDTH), CONV_K ** -0.5),
        "w_o": nrm(ks[16], (DEPTH, D, D), D ** -0.5),
        "norm2_g": 1.0 + nrm(ks[17], (DEPTH, D), 0.02),
        "w_mlp1": nrm(ks[18], (DEPTH, D, D_FF), D ** -0.5),
        "w_mlp2": nrm(ks[19], (DEPTH, D_FF, D), D_FF ** -0.5),
    }

def reference(x, norm1_g, w_in, w_gate, b_gate, a_qn_g, a_kn_g, a_rel_bias,
              b_qn_g, b_kn_g, b_lq1, b_lk1, b_lq2, b_lk2, b_subln_g, c_conv_w,
              w_o, norm2_g, w_mlp1, w_mlp2):
    B, S, _ = x.shape
    sizes = [A_WIDTH, A_WIDTH, A_WIDTH, B_QK_WIDTH, B_QK_WIDTH, B_V_WIDTH,
             C_WIDTH, C_WIDTH, C_WIDTH]
    offsets = [int(o) for o in np.cumsum(sizes)[:-1]]
    for l in range(DEPTH):
        h = _rms(x, norm1_g[l])
        proj = h @ w_in[l]
        qa, ka, va, qb, kb, vb, bg, cg, xc = jnp.split(proj, offsets, axis=-1)

        qa = _rms(qa.reshape(B, S, A_HEADS, HEAD_DIM), a_qn_g[l])
        ka = _rms(ka.reshape(B, S, A_HEADS, HEAD_DIM), a_kn_g[l])
        va = va.reshape(B, S, A_HEADS, HEAD_DIM)
        out_a = _chunked_relpos_attention(qa, ka, va, a_rel_bias[l])

        qb = _rms(qb.reshape(B, S, B_HEADS, 2, HEAD_DIM), b_qn_g[l])
        kb = _rms(kb.reshape(B, S, B_HEADS, 2, HEAD_DIM), b_kn_g[l])
        vb = vb.reshape(B, S, B_HEADS, 2 * HEAD_DIM)
        lambda_init = 0.8 - 0.6 * math.exp(-0.3 * l)
        lam = (jnp.exp(jnp.sum(b_lq1[l].astype(jnp.float32) * b_lk1[l].astype(jnp.float32)))
               - jnp.exp(jnp.sum(b_lq2[l].astype(jnp.float32) * b_lk2[l].astype(jnp.float32)))
               + lambda_init)
        ob = _differential_attention(qb[..., 0, :], qb[..., 1, :], kb[..., 0, :], kb[..., 1, :], vb, lam)
        out_b = (_rms(ob, b_subln_g[l]) * (1.0 - lambda_init)).reshape(B, S, B_V_WIDTH)

        out_c = _short_gated_conv(bg, cg, xc, c_conv_w[l])

        gates = jax.nn.sigmoid(h @ w_gate[l] + b_gate[l])
        g_a, g_b, g_c = jnp.split(gates, N_BRANCH, axis=-1)
        x = x + (g_a * out_a + g_b * out_b + g_c * out_c) @ w_o[l]

        h2 = _rms(x, norm2_g[l])
        x = x + jnp.square(jax.nn.relu(h2 @ w_mlp1[l])) @ w_mlp2[l]
    return x


_drawn_inputs = setup_inputs


def setup_inputs(seed=0):
    import zlib

    import numpy as np

    out = dict(_drawn_inputs(seed))
    spreads = {}
    factors = {'b_gate': 8.0,
     'a_qn_g': 8.0,
     'a_kn_g': 8.0,
     'a_rel_bias': 8.0,
     'b_qn_g': 6.439,
     'b_kn_g': 6.013,
     'b_subln_g': 7.569,
     'norm2_g': 3.45}
    for name, (base, spread) in spreads.items():
        noise = np.random.default_rng([zlib.crc32(name.encode()), seed]).standard_normal(out[name].shape)
        drawn = base * np.exp(spread * noise) if base else spread * noise
        out[name] = __import__('jax').numpy.asarray(drawn.astype(out[name].dtype))
    for name, factor in factors.items():
        out[name] = (out[name] * factor).astype(out[name].dtype)
    return out
```

```python
import math
from contextlib import ExitStack

import concourse.bass as bass
from concourse import mybir


def build_trunk(nc, x, norm1_g, w_in, w_gate, b_gate, a_qn_g, a_kn_g, a_rel_bias, b_qn_g, b_kn_g,
                b_lq1, b_lk1, b_lq2, b_lk2, b_subln_g, c_conv_w, w_o, norm2_g, w_mlp1, w_mlp2, out):
    F32, F32R = mybir.dt.float32, mybir.dt.float32r
    ALU, ACT, AX = mybir.AluOpType, mybir.ActivationFunctionType, mybir.AxisListType
    MUL, ADD, SUB = ALU.mult, ALU.add, ALU.subtract

    P = 128
    D = x.shape[2]
    NB = x.shape[1] // P
    T = NB * P
    N = 512
    KT = D // P
    STEPS = KT // 2
    HD = 128
    GROUPS = D // N
    NC = 12
    MAPS = N // HD
    KT4 = N // P
    CHUNK = 64
    MAX_REL = 128
    REL = a_rel_bias.shape[2]
    EXT = 384
    EPS = 1e-6
    SCALE = HD ** -0.5
    LAMBDA_INIT = 0.8 - 0.6 * math.exp(-0.3 * 0)
    NEG = -1.0e30
    RAW, RING = 4, 4
    AHEAD = RING - 1
    QUARTERS = w_mlp1.shape[2] // D
    WO0 = GROUPS * NC
    MLP0 = WO0 + GROUPS
    MC = 2 * GROUPS

    K_A, Q_A, V_A, G_A, K_B, Q_B, V_B, G_B, C_G, X_C, B_G, G_C = range(NC)
    PARTS = {K_A: (w_in, D), Q_A: (w_in, 0), V_A: (w_in, 2 * D), G_A: (w_gate, 0),
             K_B: (w_in, 4 * D), Q_B: (w_in, 3 * D), V_B: (w_in, 5 * D), G_B: (w_gate, D),
             C_G: (w_in, 7 * D), X_C: (w_in, 8 * D), B_G: (w_in, 6 * D), G_C: (w_gate, 2 * D)}

    def by_ktile(w):
        return w[0].rearrange("(k p) n -> p k n", p=P)

    ctx = ExitStack()
    with ctx:
        def sb(name, shape, dt=F32):
            return ctx.enter_context(nc.sbuf_tensor(name, shape, dt))

        def sem(name):
            return ctx.enter_context(nc.semaphore(name))

        act_in = sb("act_in", [P, 2, KT, T], F32R)
        act_mid = sb("act_mid", [P, 2, KT, T], F32R)
        raw = sb("raw", [P, RAW, 4, N])
        w_hi = sb("w_hi", [P, RING, 2, N], F32R)
        w_lo = sb("w_lo", [P, RING, 2, N], F32R)
        resid = sb("resid", [P, NB, D])
        kbuf = sb("kbuf", [P, NB, N])
        qbuf = sb("qbuf", [P, NB, N])
        vbuf = sb("vbuf", [P, NB, N])
        gbuf = sb("gbuf", [P, NB, N])
        mix = sb("mix", [P, NB, N])
        kT = sb("kT", [P, MAPS, T])
        qT = sb("qT", [P, MAPS, T])
        sbuf_s = sb("scores", [P, MAPS * 3 * P])
        pbuf = sb("pbuf", [P, 4 * N])
        rel = sb("rel", [P, MAPS, 2 * P])
        conv_w = sb("conv_w", [P, 3, N])
        gate_b = sb("gate_b", [P, 3, N])
        sub_g = sb("sub_g", [P, 2, 2 * HD])
        mask = sb("mask", [P, 2 * P])
        ident = sb("ident", [P, P])
        rel_rows = sb("rel_rows", [D // HD, EXT])
        gains = sb("gains", [P, 4])
        kq_gain = sb("kq_gain", [P, 2])
        neg_half = sb("neg_half", [P, 8])
        lam_v = vbuf[:, 0, :].rearrange("p (v d) -> p v d", v=4)
        lam2 = sb("lam2", [P, 2])
        lam_e = sb("lam_e", [P, 2])
        neg_lam = sb("neg_lam", [P, 1])
        ss_x = sb("ss_x", [P, NB, 4])
        ss_h = sb("ss_h", [P, NB, 4])
        ms_x = sb("ms_x", [P, NB])
        r_x = sb("r_x", [P, NB])
        ms_h = sb("ms_h", [P, NB])
        r_h = sb("r_h", [P, NB])
        sumsq = sb("sumsq", [P, 8])
        meansq = sb("meansq", [P, 8])
        r_k = sb("r_k", [P, 8])
        r_q = sb("r_q", [P, 8])
        neg_max = sb("neg_max", [P, 8])
        row_sum = sb("row_sum", [P, 8])
        r_sum = sb("r_sum", [P, 8])
        lam_ratio = sb("lam_ratio", [P, 4])
        ss_b = sb("ss_b", [P, 4])
        ms_b = sb("ms_b", [P, 4])
        r_b = sb("r_b", [P, 4])
        coef_b = sb("coef_b", [P, 4])
        rel_ext = nc.dram_tensor("rel_ext", (D // HD, EXT), F32, kind="Internal")

        acc = [ctx.enter_context(nc.psum_tensor(f"acc{p}", [P, NB, N], F32)) for p in range(2)]
        side = [ctx.enter_context(nc.psum_tensor(f"side{p}", [P, 2 * N], F32)) for p in range(2)]

        s3 = sbuf_s[:, :].rearrange("p (m k) -> p m k", m=MAPS)
        scratch = sbuf_s[:, 0:NB * N]
        scratch2 = scratch.rearrange("p (b n) -> p b n", b=NB)
        pT = pbuf[:, 0:12 * P].rearrange("p (t k) -> p t k", t=12)
        u1 = pbuf[:, 0:NB * N].rearrange("p (b n) -> p b n", b=NB)
        u2 = pbuf[:, NB * N:2 * NB * N].rearrange("p (b n) -> p b n", b=NB)
        scaled = [mix, gbuf]

        raw_full = [sem(f"raw_full{q}") for q in range(RAW)]
        hi_ready = sem("hi_ready")
        lo_ready = sem("lo_ready")
        step_done = sem("step_done")
        acc_read = [sem(f"acc_read{p}") for p in range(2)]
        side_full = [sem(f"side_full{p}") for p in range(2)]
        side_read = [sem(f"side_read{p}") for p in range(2)]
        act_hi = sem("act_hi")
        x_in = [sem(f"x_in{n}") for n in range(GROUPS)]
        small_in = sem("small_in")
        rel_in = sem("rel_in")
        rel_rows_done = sem("rel_rows_done")
        rel_stored = sem("rel_stored")
        rel_loaded = sem("rel_loaded")
        rel_ready = sem("rel_ready")
        taps_in = sem("taps_in")
        gateb_in = sem("gateb_in")
        gain2_in = sem("gain2_in")
        ident_set = sem("ident_set")
        ident_ready = sem("ident_ready")
        mask_set = sem("mask_set")
        mask_ready = sem("mask_ready")
        half_ready = sem("half_ready")
        x_scaled = sem("x_scaled")
        x_squared = sem("x_squared")
        ssx_done = sem("ssx_done")
        msx_done = sem("msx_done")
        rx_done = sem("rx_done")
        kq_gain_done = sem("kq_gain_done")
        lam_prod = sem("lam_prod")
        lam_sum = sem("lam_sum")
        lam_exp = sem("lam_exp")
        lam_diff = sem("lam_diff")
        lam_done = sem("lam_done")
        sq_done = sem("sq_done")
        ss_done = sem("ss_done")
        ms_done = sem("ms_done")
        rstd_done = sem("rstd_done")
        kn_done = sem("kn_done")
        max_done = sem("max_done")
        exp_done = sem("exp_done")
        rsum_done = sem("rsum_done")
        ratio_done = sem("ratio_done")
        comb_done = sem("comb_done")
        gate_done = sem("gate_done")
        ssb_done = sem("ssb_done")
        msb_done = sem("msb_done")
        rstdb_done = sem("rstdb_done")
        coefb_done = sem("coefb_done")
        outb_done = sem("outb_done")
        outb_gated = sem("outb_gated")
        mixb_done = sem("mixb_done")
        zero_rows = sem("zero_rows")
        shifted = sem("shifted")
        taps_done = sem("taps_done")
        tap_sum = sem("tap_sum")
        conv_done = sem("conv_done")
        gated_c = sem("gated_c")
        mix_done = sem("mix_done")
        x1_scaled = sem("x1_scaled")
        x1_squared = sem("x1_squared")
        ssh_done = sem("ssh_done")
        msh_done = sem("msh_done")
        rh_done = sem("rh_done")
        hid_squared = sem("hid_squared")
        stored = sem("stored")

        def chunk_of(g, c):
            return g * NC + c

        SIDE = [["kT_a", "scores_a", "pT_a", "kT_b", "scores_b", "pT_b", "mixT"],
                ["qT_a", "scores_a", "pT_a", "out_a", "qT_b", "scores_b", "out_b"]]
        FIRST_SIDE = GROUPS // 2

        def side_no(p, g, name):
            return g * len(SIDE[p]) + (FIRST_SIDE + SIDE[p].index(name) + 1)

        H2_SIDE = FIRST_SIDE + GROUPS * len(SIDE[0])
        HID_SIDE = H2_SIDE + GROUPS

        def acc_no(chunk_g, per, c):
            return chunk_g * (per // 2) + (c // 2 + 1)

        def read_no(chunk):
            return chunk // 2 + 1

        def ab(c):
            return 0 if c < K_B else 1

        block = ctx.enter_context(nc.Block())

        @block.sync
        def _(sp):
            def column(g, col=0):
                return g * N + col if isinstance(g, int) else (g + 1) * N + (col - N)

            def load_weights(w, chunk, n0):
                for q in range(RAW):
                    sp.wait_ge(lo_ready, (chunk - 1) * STEPS + 2 * q + 2)
                    sp.dma_start(raw[:, q, :, :], by_ktile(w)[:, 4 * q:4 * q + 4, bass.ds(n0, N)]) \
                        .then_inc(raw_full[q], 16)

            def load_down(w, chunk, f, n):
                wk = w[0].rearrange("(k p) n -> p k n", p=P)
                for q in range(RAW):
                    sp.wait_ge(lo_ready, (chunk - 1) * STEPS + 2 * q + 2)
                    sp.dma_start(raw[:, q, :, :], wk[:, bass.ds(f * KT + 4 * q, 4), n * N:(n + 1) * N]) \
                        .then_inc(raw_full[q], 16)

            def load_group_constants(g):
                first = isinstance(g, int) and g == 0
                if first:
                    sp.wait_ge(rel_stored, 16)
                else:
                    sp.wait_ge(side_read[1], side_no(1, g - 1, "scores_a"))
                sp.dma_start(rel[:, :, :], bass.AP(rel_ext, g * (MAPS * EXT) + 1,
                                                   [[1, P], [EXT, MAPS], [1, 2 * P]])) \
                    .then_inc(rel_loaded, 16)
                if not first:
                    sp.wait_ge(conv_done, g + 1)
                taps = c_conv_w[0, :, bass.ds(column(g), N)]
                sp.dma_start(conv_w[:, :, :], taps.partition_broadcast(P)).then_inc(taps_in, 16)
                if not first:
                    sp.wait_ge(gate_done, g * 3)
                bias = b_gate[0, :].rearrange("(j n) -> j n", j=3)[:, bass.ds(column(g), N)]
                sp.dma_start(gate_b[:, :, :], bias.partition_broadcast(P)).then_inc(gateb_in, 16)

            def group_chunks(g, chunks):
                for c in chunks:
                    if c == 1 and not (isinstance(g, int) and g == 0):
                        load_group_constants(g)
                    w, col = PARTS[c]
                    load_weights(w, chunk_of(g, c), column(g, col))

            xr = x[0].rearrange("(b p) d -> p b d", p=P)
            w, col = PARTS[0]
            for n in range(GROUPS):
                cols = slice(n * N, (n + 1) * N)
                sp.dma_start(resid[:, :, cols], xr[:, :, cols]).then_inc(x_in[n], 16)
                sp.dma_start(pbuf[:, cols], norm1_g[0, cols].partition_broadcast(P)).then_inc(x_in[n], 16)
                sp.dma_start(raw[:, n, :, :], by_ktile(w)[:, 4 * n:4 * n + 4, col:col + N]) \
                    .then_inc(raw_full[n], 16)
            group_chunks(0, [1])
            load_group_constants(0)
            with sp.Fori(0, GROUPS - 1) as i:
                group_chunks(i, range(2, NC))
                group_chunks(i + 1, range(2))
            group_chunks(GROUPS - 1, range(2, NC))
            for n in range(GROUPS):
                load_weights(w_o, WO0 + n, n * N)
                if n == 0:
                    sp.wait_ge(conv_done, GROUPS + 1)
                    sp.dma_start(pbuf[:, :], norm2_g[0, :].partition_broadcast(P)).then_inc(gain2_in, 16)

            def quarter(f):
                for j in range(GROUPS):
                    load_weights(w_mlp1, f * MC + (MLP0 + j), f * D + j * N)
                for n in range(GROUPS):
                    load_down(w_mlp2, f * MC + (MLP0 + GROUPS + n), f, n)

            with sp.Fori(0, QUARTERS) as f:
                quarter(f)
            outr = out[0].rearrange("(b p) d -> p b d", p=P)
            for n in range(GROUPS):
                last = MLP0 + QUARTERS * MC - GROUPS + n
                sp.wait_ge(acc_read[last % 2], read_no(last))
                sp.dma_start(outr[:, :, n * N:(n + 1) * N], resid[:, :, n * N:(n + 1) * N]) \
                    .then_inc(stored, 16)
            sp.wait_ge(stored, 16 * GROUPS)

        @block.tensor
        def _(pe):
            def transpose_tile(pair, src):
                for t in range(KT4):
                    for b in range(NB):
                        last = nc.tensor.transpose(side[pair][:, t * T + b * P:t * T + (b + 1) * P],
                                                   src[:, b, t * P:(t + 1) * P], ident[:, :])
                return last

            def step(chunk, parity, s, act):
                pe.wait_ge(lo_ready, chunk * STEPS + (s + 1))
                for kk in range(2):
                    k = 2 * s + kk
                    for b in range(NB):
                        xh, xl = (act[:, part, k, b * P:(b + 1) * P] for part in range(2))
                        wh, wl = w_hi[:, s % RING, kk, :], w_lo[:, s % RING, kk, :]
                        o = acc[parity][:, b, :]
                        nc.tensor.matmul(o, xh, wh, start=(k == 0), stop=False)
                        nc.tensor.matmul(o, xh, wl, start=False, stop=False)
                        last = nc.tensor.matmul(o, xl, wh, start=False, stop=(k == KT - 1))
                last.then_inc(step_done, 1)

            def free_acc(g, per, c):
                pe.wait_ge(acc_read[c % 2], acc_no(g, per, c) - 1)

            def start_side(pair, no):
                pe.wait_ge(side_read[pair], no - 1)

            def transpose_keys(g, c):
                no = side_no(0, g, "kT_a" if c == K_A else "kT_b")
                start_side(0, no)
                pe.wait_ge(kn_done, g * 2 + (ab(c) + 1))
                for m in range(MAPS):
                    for b in range(NB):
                        last = nc.tensor.transpose(side[0][:, m * T + b * P:m * T + (b + 1) * P],
                                                   kbuf[:, b, m * HD:(m + 1) * HD], ident[:, :])
                last.then_inc(side_full[0], 1)

            def transpose_queries(g, c):
                no = side_no(1, g, "qT_a" if c == Q_A else "qT_b")
                start_side(1, no)
                pe.wait_ge(acc_read[c % 2], acc_no(g, NC, c))
                for m in range(MAPS):
                    for b in range(NB):
                        last = nc.tensor.transpose(side[1][:, m * T + b * P:m * T + (b + 1) * P],
                                                   qbuf[:, b, m * HD:(m + 1) * HD], ident[:, :])
                last.then_inc(side_full[1], 1)

            def scores(g, br):
                name = "scores_" + br
                pe.wait_ge(side_read[0], side_no(0, g, "kT_" + br))
                pe.wait_ge(side_read[1], side_no(1, g, "qT_" + br))
                for m in range(MAPS):
                    last = nc.tensor.matmul(side[0][:, m * T:(m + 1) * T], qT[:, m, P:T], kT[:, m, :],
                                            start=True, stop=True)
                last.then_inc(side_full[0], 1)
                for m in range(MAPS):
                    last = nc.tensor.matmul(side[1][:, m * P:(m + 1) * P], qT[:, m, 0:P], kT[:, m, 0:P],
                                            start=True, stop=True)
                last.then_inc(side_full[1], 1)

            def transpose_probs_a(g):
                start_side(1, side_no(1, g, "pT_a"))
                start_side(0, side_no(0, g, "pT_a"))
                pe.wait_ge(exp_done, g * 2 + 1)
                for t in list(range(8, 12)) + list(range(8)):
                    m, part = t // 3, t % 3
                    o = side[t // 8][:, (t % 8) * P:(t % 8 + 1) * P]
                    last = nc.tensor.transpose(o, s3[:, m, part * P:(part + 1) * P], ident[:, :])
                    if t == 11:
                        last.then_inc(side_full[1], 1)
                last.then_inc(side_full[0], 1)

            def transpose_probs_b(g):
                start_side(0, side_no(0, g, "pT_b"))
                pe.wait_ge(comb_done, g + 1)
                for t in range(6):
                    m, part = 2 * (t // 3), t % 3
                    last = nc.tensor.transpose(side[0][:, t * P:(t + 1) * P],
                                               s3[:, m, part * P:(part + 1) * P], ident[:, :])
                last.then_inc(side_full[0], 1)

            def values(g, br, heads, width):
                start_side(1, side_no(1, g, "out_" + br))
                pe.wait_ge(side_read[0], side_no(0, g, "pT_" + br))
                c = V_A if br == "a" else V_B
                pe.wait_ge(acc_read[c % 2], acc_no(g, NC, c))
                for h in range(heads):
                    cols = slice(h * width, (h + 1) * width)
                    nc.tensor.matmul(side[1][:, cols], pT[:, 3 * h + 2, :], vbuf[:, 0, cols],
                                     start=True, stop=True)
                    o = side[1][:, N + h * width:N + (h + 1) * width]
                    nc.tensor.matmul(o, pT[:, 3 * h, :], vbuf[:, 0, cols], start=True, stop=False)
                    last = nc.tensor.matmul(o, pT[:, 3 * h + 1, :], vbuf[:, 1, cols],
                                            start=False, stop=True)
                last.then_inc(side_full[1], 1)

            def transpose_mix(g):
                start_side(0, side_no(0, g, "mixT"))
                pe.wait_ge(mix_done, g + 1)
                transpose_tile(0, mix).then_inc(side_full[0], 1)

            def group_chunks(g, chunks):
                first = isinstance(g, int) and g == 0
                for c in chunks:
                    for s in range(STEPS):
                        if s == 0 and not (first and c < 2):
                            free_acc(g, NC, c)
                        if (c, s) == (0, 5) and not first:
                            transpose_mix(g - 1)
                        elif (c, s) == (1, 5):
                            transpose_keys(g, K_A)
                        elif (c, s) == (2, 2):
                            transpose_queries(g, Q_A)
                        elif (c, s) == (3, 0):
                            scores(g, "a")
                        elif (c, s) == (4, 1):
                            transpose_probs_a(g)
                        elif (c, s) == (4, 5):
                            values(g, "a", MAPS, HD)
                        elif (c, s) == (5, 5):
                            transpose_keys(g, K_B)
                        elif (c, s) == (6, 2):
                            transpose_queries(g, Q_B)
                        elif (c, s) == (7, 0):
                            scores(g, "b")
                        elif (c, s) == (8, 1):
                            transpose_probs_b(g)
                        elif (c, s) == (8, 4):
                            values(g, "b", MAPS // 2, 2 * HD)
                        if first and c == 0:
                            if s % 2 == 0:
                                pe.wait_ge(side_read[s // 2 % 2], s // 4 + 1)
                            if s == 1:
                                transpose_x(1)
                            elif s == 2:
                                transpose_x(2)
                            elif s == 4:
                                transpose_x(3)
                        step(chunk_of(g, c), c % 2, s, act_in)

            def transpose_x(n):
                if n >= 2:
                    start_side(n % 2, n // 2 + 1)
                pe.wait_ge(x_scaled, n + 1)
                transpose_tile(n % 2, scaled[n % 2]).then_inc(side_full[n % 2], 1)

            pe.wait_ge(ident_ready, 1)
            transpose_x(0)
            group_chunks(0, range(2))
            with pe.Fori(0, GROUPS - 1) as i:
                group_chunks(i, range(2, NC))
                group_chunks(i + 1, range(2))
            group_chunks(GROUPS - 1, range(2, NC))

            def transpose_h2(n):
                start_side(0, H2_SIDE + n + 1)
                pe.wait_ge(x1_scaled, n + 1)
                transpose_tile(0, gbuf).then_inc(side_full[0], 1)

            for n in range(GROUPS):
                for s in range(STEPS):
                    if s == 0:
                        free_acc(0, 2, WO0 + n)
                        if n == 0:
                            pe.wait_ge(side_read[0], side_no(0, GROUPS - 2, "mixT"))
                    if (n, s) == (0, 5):
                        transpose_mix(GROUPS - 1)
                    if (n, s) == (0, 6):
                        pe.wait_ge(side_read[0], side_no(0, GROUPS - 1, "mixT"))
                    if n > 0 and s == 3:
                        transpose_h2(n - 1)
                    step(WO0 + n, n % 2, s, act_mid)

            def transpose_hidden(f, j):
                start_side(0, f * GROUPS + (HID_SIDE + j + 1))
                pe.wait_ge(acc_read[j % 2], f * (MC // 2) + read_no(MLP0 + j))
                transpose_tile(0, qbuf).then_inc(side_full[0], 1)

            def quarter_chunks(f, chunks):
                first = isinstance(f, int) and f == 0
                for j in chunks:
                    for s in range(STEPS):
                        if s == 0:
                            pe.wait_ge(acc_read[j % 2], f * (MC // 2) + (MLP0 + j) // 2)
                        if first and j == 0:
                            if s == 0:
                                pe.wait_ge(side_read[0], H2_SIDE + GROUPS - 1)
                            elif s == 3:
                                transpose_h2(GROUPS - 1)
                            elif s == 6:
                                pe.wait_ge(side_read[0], H2_SIDE + GROUPS)
                        if 1 <= j <= GROUPS and s == 2:
                            transpose_hidden(f, j - 1)
                        if j == GROUPS and s == 0:
                            pe.wait_ge(side_read[0], f * GROUPS + (HID_SIDE + GROUPS - 1))
                        if j == GROUPS and s == 6:
                            pe.wait_ge(side_read[0], f * GROUPS + (HID_SIDE + GROUPS))
                        step(f * MC + (MLP0 + j), j % 2, s, act_in if j < GROUPS else act_mid)

            quarter_chunks(0, [0])
            with pe.Fori(0, QUARTERS - 1) as i:
                quarter_chunks(i, range(1, MC))
                quarter_chunks(i + 1, [0])
            quarter_chunks(QUARTERS - 1, range(1, MC))

        @block.scalar
        def _(act):
            def round_weights(chunk, i, reuse=True):
                q, half = i % STEPS // 2, i % 2
                act.wait_ge(raw_full[q], (chunk + i // STEPS) * 16 + 16)
                if reuse:
                    act.wait_ge(step_done, chunk * STEPS + (i - RING + 1))
                nc.scalar.activation(w_hi[:, i % RING, :, :], raw[:, q, 2 * half:2 * half + 2, :],
                                     ACT.Copy).then_inc(hi_ready, 1)

            def result_of(chunk):
                act.wait_ge(step_done, chunk * STEPS + STEPS)

            def evacuate(g, c, dst):
                result_of(chunk_of(g, c))
                nc.scalar.activation(dst[:, 0, :], acc[c % 2][:, 0, :], ACT.Copy, scale=r_x[:, 0:1])
                nc.scalar.activation(dst[:, 1, :], acc[c % 2][:, 1, :], ACT.Copy, scale=r_x[:, 1:2]) \
                    .then_inc(acc_read[c % 2], 1)

            def keys_out(g, br):
                act.wait_ge(side_full[0], side_no(0, g, "kT_" + br))
                i = "ab".index(br)
                nc.scalar.activation(kT[:, :, :], side[0][:, :].rearrange("p (m t) -> p m t", m=MAPS),
                                     ACT.Copy, scale=kq_gain[:, i:i + 1]).then_inc(side_read[0], 1)

            def queries_out(g, br):
                act.wait_ge(side_full[1], side_no(1, g, "qT_" + br))
                nc.scalar.activation(qT[:, :, :], side[1][:, :].rearrange("p (m t) -> p m t", m=MAPS),
                                     ACT.Copy).then_inc(side_read[1], 1)

            def exponentials(g, br, b):
                if b == 1:
                    act.wait_ge(max_done, g * 2 + ("ab".index(br) + 1))
                cols = slice(0, T) if b == 1 else slice(T, T + P)
                for m in range(MAPS):
                    i = b * MAPS + m
                    last = nc.scalar.activation(s3[:, m, cols], s3[:, m, cols], ACT.Exp,
                                                bias=neg_max[:, i:i + 1], accum_out=row_sum[:, i:i + 1])
                if b == 0:
                    last.then_inc(exp_done, 1)

            def gate(g, c):
                act.wait_ge(acc_read[c % 2], acc_no(g, NC, c))
                nc.scalar.activation(gbuf[:, :, :], gbuf[:, :, :], ACT.Sigmoid).then_inc(gate_done, 1)

            def probs_out(g, br, tiles):
                act.wait_ge(side_full[0], side_no(0, g, "pT_" + br))
                nc.scalar.activation(pT[:, 0:tiles, :],
                                     side[0][:, 0:tiles * P].rearrange("p (t k) -> p t k", k=P),
                                     ACT.Copy).then_inc(side_read[0], 1)

            def square_sums_b(g):
                act.wait_ge(side_full[1], side_no(1, g, "out_b"))
                act.wait_ge(rsum_done, g * 2 + 2)
                for b in range(NB):
                    for h in range(2):
                        i = 2 * b + h
                        m = MAPS * b + 2 * h
                        cols = slice(b * N + h * 2 * HD, b * N + (h + 1) * 2 * HD)
                        last = nc.scalar.activation(scratch[:, cols], side[1][:, cols], ACT.Square,
                                                    scale=r_sum[:, m:m + 1],
                                                    accum_out=ss_b[:, i:i + 1])
                last.then_inc(ssb_done, 1)

            def shift_u(g):
                act.wait_ge(acc_read[X_C % 2], acc_no(g, NC, X_C))
                act.wait_ge(zero_rows, g + 1)
                for d, dst in ((1, u1), (2, u2)):
                    act.dma_start(dst[d:P, :, :], kbuf[0:P - d, :, :]).then_inc(shifted, 16)
                    act.dma_start(dst[0:d, 1, :], kbuf[P - d:P, 0, :]).then_inc(shifted, 16)

            def split_high(pair, no, dst, n):
                act.wait_ge(side_full[pair], no)
                nc.scalar.activation(dst[:, 0, bass.ds(n * KT4, KT4), :],
                                     side[pair][:, :].rearrange("p (t k) -> p t k", t=KT4),
                                     ACT.Copy).then_inc(act_hi, 1)

            def group_chunks(g, chunks):
                first = isinstance(g, int) and g == 0
                for c in chunks:
                    for s in range(STEPS):
                        round_weights(chunk_of(g, c), s + AHEAD, reuse=not (first and c == 0 and s == 0))
                        if c == 0 and first:
                            if s == 1:
                                split_high(1, 1, act_in, 1)
                                x_squares(1)
                            elif s == 2:
                                split_high(0, 2, act_in, 2)
                            elif s == 3:
                                x_squares(2)
                            elif s == 4:
                                split_high(1, 2, act_in, 3)
                            elif s == 5:
                                x_squares(3)
                        if c == 0 and not first:
                            if s == 1:
                                gate(g - 1, G_C)
                            elif s == 5:
                                split_high(0, side_no(0, g - 1, "mixT"), act_mid, g - 1)
                        if (c, s) == (1, 0):
                            evacuate(g, K_A, kbuf)
                        elif (c, s) == (1, 6):
                            keys_out(g, "a")
                        elif (c, s) == (2, 0):
                            evacuate(g, Q_A, qbuf)
                        elif (c, s) == (2, 3):
                            queries_out(g, "a")
                        elif (c, s) == (3, 0):
                            evacuate(g, V_A, vbuf)
                        elif (c, s) == (3, 4):
                            exponentials(g, "a", 1)
                        elif (c, s) == (3, 5):
                            exponentials(g, "a", 0)
                        elif (c, s) == (4, 1):
                            gate(g, G_A)
                        elif (c, s) == (4, 2):
                            act.wait_ge(conv_done, g + 1)
                            probs_out(g, "a", 8)
                        elif (c, s) == (5, 0):
                            evacuate(g, K_B, kbuf)
                        elif (c, s) == (5, 6):
                            keys_out(g, "b")
                        elif (c, s) == (6, 0):
                            evacuate(g, Q_B, qbuf)
                        elif (c, s) == (6, 3):
                            queries_out(g, "b")
                        elif (c, s) == (7, 0):
                            evacuate(g, V_B, vbuf)
                        elif (c, s) == (7, 4):
                            exponentials(g, "b", 1)
                        elif (c, s) == (7, 5):
                            exponentials(g, "b", 0)
                        elif (c, s) == (8, 1):
                            gate(g, G_B)
                        elif (c, s) == (8, 2):
                            probs_out(g, "b", 6)
                        elif (c, s) == (8, 5):
                            square_sums_b(g)
                        elif (c, s) == (9, 0):
                            evacuate(g, C_G, kbuf)
                        elif (c, s) == (10, 1):
                            shift_u(g)

            def x_squares(n):
                act.wait_ge(x_in[n], 32)
                if n > 0:
                    act.wait_ge(x_squared, n)
                for b in range(NB):
                    last = nc.scalar.activation(scratch2[:, b, :], resid[:, b, n * N:(n + 1) * N],
                                                ACT.Square, accum_out=ss_x[:, b, n:n + 1])
                last.then_inc(x_squared, 1)

            round_weights(0, 0, reuse=False)
            split_high(0, 1, act_in, 0)
            round_weights(0, 1, reuse=False)
            x_squares(0)
            round_weights(0, 2, reuse=False)
            group_chunks(0, [0])
            act.wait_ge(lam_sum, 1)
            nc.scalar.activation(lam_e[:, :], lam2[:, :], ACT.Exp).then_inc(lam_exp, 1)
            act.wait_ge(rx_done, 1)
            act.wait_ge(kq_gain_done, 2)
            group_chunks(0, [1])
            with act.Fori(0, GROUPS - 1) as i:
                group_chunks(i, range(2, NC))
                group_chunks(i + 1, range(2))
            group_chunks(GROUPS - 1, range(2, NC))

            def x1_squares(n):
                act.wait_ge(acc_read[n % 2], read_no(WO0 + n))
                if n > 0:
                    act.wait_ge(x1_squared, n)
                for b in range(NB):
                    last = nc.scalar.activation(scratch2[:, b, :], resid[:, b, n * N:(n + 1) * N],
                                                ACT.Square, accum_out=ss_h[:, b, n:n + 1])
                last.then_inc(x1_squared, 1)

            for n in range(GROUPS):
                for s in range(STEPS):
                    round_weights(WO0 + n, s + AHEAD)
                    if (n, s) == (0, 1):
                        gate(GROUPS - 1, G_C)
                    elif (n, s) == (0, 5):
                        split_high(0, side_no(0, GROUPS - 1, "mixT"), act_mid, GROUPS - 1)
                    elif n > 0 and s == 1:
                        x1_squares(n - 1)
                    elif n > 0 and s == 3:
                        split_high(0, H2_SIDE + n, act_in, n - 1)

            def relu_out(f, j):
                result_of(f * MC + (MLP0 + j))
                for b in range(NB):
                    last = nc.scalar.activation(qbuf[:, b, :], acc[j % 2][:, b, :], ACT.Relu,
                                                scale=r_h[:, b:b + 1])
                last.then_inc(acc_read[j % 2], 1)

            def square_hidden(f, j):
                act.wait_ge(side_full[0], f * GROUPS + (HID_SIDE + j + 1))
                nc.scalar.activation(kbuf[:, :, :], side[0][:, :].rearrange("p (b n) -> p b n", b=NB),
                                     ACT.Square).then_inc(hid_squared, 1)

            def hidden_high(f, j):
                act.wait_ge(hid_squared, f * GROUPS + (j + 1))
                nc.scalar.activation(act_mid[:, 0, j * KT4:(j + 1) * KT4, :],
                                     kbuf[:, :, :].rearrange("p b (t k) -> p (b t) k", k=T),
                                     ACT.Copy).then_inc(act_hi, 1)

            def quarter_chunks(f, chunks, last_quarter=False):
                first = isinstance(f, int) and f == 0
                for j in chunks:
                    for s in range(STEPS):
                        if not (last_quarter and j == MC - 1 and s + AHEAD >= STEPS):
                            round_weights(f * MC + (MLP0 + j), s + AHEAD)
                        if first and j == 0:
                            if s == 1:
                                x1_squares(GROUPS - 1)
                            elif s == 3:
                                split_high(0, H2_SIDE + GROUPS, act_in, GROUPS - 1)
                        if 1 <= j <= GROUPS:
                            if s == 0:
                                relu_out(f, j - 1)
                            elif s == 3:
                                square_hidden(f, j - 1)
                                hidden_high(f, j - 1)

            quarter_chunks(0, [0])
            act.wait_ge(rh_done, 1)
            with act.Fori(0, QUARTERS - 1) as i:
                quarter_chunks(i, range(1, MC))
                quarter_chunks(i + 1, [0])
            quarter_chunks(QUARTERS - 1, range(1, MC), last_quarter=True)

        @block.vector
        def _(dve):
            def low_weights(chunk, i, reuse=True):
                q, half = i % STEPS // 2, i % 2
                dve.wait_ge(hi_ready, chunk * STEPS + (i + 1))
                if reuse:
                    dve.wait_ge(step_done, chunk * STEPS + (i - RING + 1))
                nc.vector.tensor_tensor(w_lo[:, i % RING, :, :], raw[:, q, 2 * half:2 * half + 2, :],
                                        w_hi[:, i % RING, :, :].bitcast(F32), SUB).then_inc(lo_ready, 1)

            def result_of(chunk):
                dve.wait_ge(step_done, chunk * STEPS + STEPS)

            def mean_squares(g, e):
                dve.wait_ge(sq_done, g * 4 + (e + 1))
                nc.vector.tensor_reduce(sumsq[:, :], scratch.rearrange("p (i d) -> p i d", d=HD),
                                        AX.X, ADD).then_inc(ss_done, 1)
                dve.wait_ge(ss_done, g * 4 + (e + 1))
                nc.vector.tensor_scalar(meansq[:, :], sumsq[:, :], 1.0 / HD, EPS, MUL, ADD) \
                    .then_inc(ms_done, 1)

            def biased_scores(g, br, b):
                if b == 1:
                    dve.wait_ge(rstd_done, g * 4 + (2 if br == "a" else 4))
                    if br == "a":
                        dve.wait_ge(rel_ready, g + 1)
                pair, width = (0, T) if b == 1 else (1, P)
                dve.wait_ge(side_full[pair], side_no(pair, g, "scores_" + br))
                for m in range(MAPS):
                    if br == "a":
                        add = rel[:, m, width - 1::-1]
                    else:
                        add = mask[:, T - width:T]
                    o = s3[:, m, 0:T] if b == 1 else s3[:, m, T:T + P]
                    i = b * MAPS + m
                    last = nc.vector.scalar_tensor_tensor(
                        out=o, in0=side[pair][:, m * width:(m + 1) * width], scalar=r_q[:, i:i + 1],
                        in1=add, op0=MUL, op1=ADD)
                last.then_inc(side_read[pair], 1)

            def row_max(g, br):
                dve.wait_ge(side_read[1], side_no(1, g, "scores_" + br))
                nc.vector.tensor_reduce(neg_max[:, MAPS:2 * MAPS], s3[:, :, 0:T], AX.X, ALU.max,
                                        negate=True)
                nc.vector.tensor_reduce(neg_max[:, 0:MAPS], s3[:, :, T:T + P], AX.X, ALU.max,
                                        negate=True).then_inc(max_done, 1)

            def row_reciprocals(g, br):
                i = "ab".index(br)
                dve.wait_ge(exp_done, g * 2 + (i + 1))
                nc.vector.reciprocal(r_sum[:, :], row_sum[:, :]).then_inc(rsum_done, 1)

            def difference(g):
                dve.wait_ge(rsum_done, g * 2 + 2)
                pairs = row_sum[:, :].rearrange("p (i two) -> p i two", two=2)
                rpairs = r_sum[:, :].rearrange("p (i two) -> p i two", two=2)
                nc.vector.scalar_tensor_tensor(out=lam_ratio[:, :], in0=pairs[:, :, 0],
                                               scalar=neg_lam[:, 0:1], in1=rpairs[:, :, 1],
                                               op0=MUL, op1=MUL).then_inc(ratio_done, 1)
                dve.wait_ge(ratio_done, g + 1)
                for b in range(NB):
                    cols = slice(0, T) if b == 1 else slice(T, T + P)
                    for h in range(2):
                        i = 2 * b + h
                        last = nc.vector.scalar_tensor_tensor(
                            out=s3[:, 2 * h, cols], in0=s3[:, 2 * h + 1, cols],
                            scalar=lam_ratio[:, i:i + 1], in1=s3[:, 2 * h, cols], op0=MUL, op1=ADD)
                last.then_inc(comb_done, 1)

            def gate_sum(g, c, j):
                result_of(chunk_of(g, c))
                dve.wait_ge(gateb_in, g * 16 + 16)
                for b in range(NB):
                    last = nc.vector.scalar_tensor_tensor(
                        out=gbuf[:, b, :], in0=acc[c % 2][:, b, :], scalar=r_x[:, b:b + 1],
                        in1=gate_b[:, j, :], op0=MUL, op1=ADD)
                last.then_inc(acc_read[c % 2], 1)

            def probs_out_a(g):
                dve.wait_ge(side_full[1], side_no(1, g, "pT_a"))
                nc.vector.tensor_copy(pT[:, 8:12, :], side[1][:, 0:N].rearrange("p (t k) -> p t k", k=P)) \
                    .then_inc(side_read[1], 1)

            def out_a(g, b):
                if b == 0:
                    dve.wait_ge(side_full[1], side_no(1, g, "out_a"))
                    dve.wait_ge(gate_done, g * 3 + 1)
                    dve.wait_ge(rsum_done, g * 2 + 1)
                for m in range(MAPS):
                    cols = slice(m * HD, (m + 1) * HD)
                    i = b * MAPS + m
                    last = nc.vector.scalar_tensor_tensor(
                        out=mix[:, b, cols], in0=side[1][:, b * N + m * HD:b * N + (m + 1) * HD],
                        scalar=r_sum[:, i:i + 1], in1=gbuf[:, b, cols], op0=MUL, op1=MUL)
                if b == 1:
                    last.then_inc(side_read[1], 1)

            def mean_squares_b(g):
                dve.wait_ge(ssb_done, g + 1)
                nc.vector.tensor_scalar(ms_b[:, :], ss_b[:, :], 1.0 / (2 * HD), EPS, MUL, ADD) \
                    .then_inc(msb_done, 1)

            def out_b(g):
                dve.wait_ge(rstdb_done, g + 1)
                first_sums = r_sum[:, :].rearrange("p (i two) -> p i two", two=2)[:, :, 0]
                nc.vector.tensor_tensor(coef_b[:, :], first_sums, r_b[:, :], MUL).then_inc(coefb_done, 1)
                dve.wait_ge(coefb_done, g + 1)
                for b in range(NB):
                    for h in range(2):
                        i = 2 * b + h
                        cols = slice(b * N + h * 2 * HD, b * N + (h + 1) * 2 * HD)
                        last = nc.vector.scalar_tensor_tensor(
                            out=scratch[:, cols], in0=side[1][:, cols], scalar=coef_b[:, i:i + 1],
                            in1=sub_g[:, h, :], op0=MUL, op1=MUL)
                last.then_inc(side_read[1], 1)

            def times(g, c, dst):
                result_of(chunk_of(g, c))
                for b in range(NB):
                    last = nc.vector.scalar_tensor_tensor(
                        out=dst[:, b, :], in0=acc[c % 2][:, b, :], scalar=r_x[:, b:b + 1],
                        in1=dst[:, b, :], op0=MUL, op1=MUL)
                last.then_inc(acc_read[c % 2], 1)

            def add_c(g):
                dve.wait_ge(gate_done, g * 3 + 3)
                dve.wait_ge(acc_read[B_G % 2], acc_no(g, NC, B_G))
                nc.vector.tensor_tensor(kbuf[:, :, :], kbuf[:, :, :], gbuf[:, :, :], MUL) \
                    .then_inc(gated_c, 1)
                dve.wait_ge(gated_c, g + 1)
                dve.wait_ge(mixb_done, g + 1)
                nc.vector.tensor_tensor(mix[:, :, :], mix[:, :, :], kbuf[:, :, :], ADD) \
                    .then_inc(mix_done, 1)

            def split_low(pair, no, hi_no, dst, n):
                dve.wait_ge(side_full[pair], no)
                dve.wait_ge(act_hi, hi_no)
                tiles = bass.ds(n * KT4, KT4)
                nc.vector.tensor_tensor(dst[:, 1, tiles, :],
                                        side[pair][:, :].rearrange("p (t k) -> p t k", t=KT4),
                                        dst[:, 0, tiles, :].bitcast(F32), SUB).then_inc(side_read[pair], 1)

            def group_chunks(g, chunks):
                first = isinstance(g, int) and g == 0
                for c in chunks:
                    for s in range(STEPS):
                        low_weights(chunk_of(g, c), s + AHEAD, reuse=not (first and c == 0 and s == 0))
                        if c == 0 and first:
                            if s == 0:
                                scale_x(2)
                            elif s == 1:
                                split_low(1, 1, 2, act_in, 1)
                            elif s == 2:
                                scale_x(3)
                                split_low(0, 2, 3, act_in, 2)
                            elif s == 3:
                                extend_rel_rows()
                            elif s == 4:
                                split_low(1, 2, 4, act_in, 3)
                            elif s == 5:
                                prepare_gains()
                            elif s == 6:
                                mean_squares_x()
                            elif s == 7:
                                lambda_products()
                        if first and (c, s) == (1, 0):
                            negative_lambda()
                            dve.wait_ge(rx_done, 1)
                        if c == 0 and not first:
                            if s == 0:
                                dve.wait_ge(mixb_done, g)
                                gate_sum(g - 1, G_C, 2)
                            elif s == 3:
                                add_c(g - 1)
                            elif s == 6:
                                split_low(0, side_no(0, g - 1, "mixT"), g + GROUPS, act_mid, g - 1)
                        if (c, s) == (1, 2):
                            mean_squares(g, 0)
                        elif (c, s) == (2, 2):
                            mean_squares(g, 1)
                        elif (c, s) == (3, 1):
                            biased_scores(g, "a", 1)
                        elif (c, s) == (3, 2):
                            biased_scores(g, "a", 0)
                        elif (c, s) == (3, 3):
                            row_max(g, "a")
                        elif (c, s) == (3, 7):
                            row_reciprocals(g, "a")
                        elif (c, s) == (4, 0):
                            gate_sum(g, G_A, 0)
                        elif (c, s) == (4, 2):
                            dve.wait_ge(conv_done, g + 1)
                            probs_out_a(g)
                        elif (c, s) == (4, 6):
                            out_a(g, 0)
                        elif (c, s) == (4, 7):
                            out_a(g, 1)
                        elif (c, s) == (5, 2):
                            mean_squares(g, 2)
                        elif (c, s) == (6, 2):
                            mean_squares(g, 3)
                        elif (c, s) == (7, 1):
                            biased_scores(g, "b", 1)
                        elif (c, s) == (7, 2):
                            biased_scores(g, "b", 0)
                        elif (c, s) == (7, 3):
                            row_max(g, "b")
                        elif (c, s) == (7, 7):
                            row_reciprocals(g, "b")
                            difference(g)
                        elif (c, s) == (8, 0):
                            gate_sum(g, G_B, 1)
                        elif (c, s) == (8, 6):
                            mean_squares_b(g)
                        elif (c, s) == (9, 0):
                            out_b(g)
                        elif (c, s) == (10, 0):
                            dve.wait_ge(acc_read[C_G % 2], acc_no(g, NC, C_G))
                            times(g, X_C, kbuf)
                        elif (c, s) == (11, 0):
                            dve.wait_ge(conv_done, g + 2)
                            times(g, B_G, kbuf)

            def scale_x(n):
                dve.wait_ge(x_in[n], 32)
                if n >= 2:
                    dve.wait_ge(side_full[n % 2], n // 2)
                for b in range(NB):
                    last = nc.vector.tensor_tensor(scaled[n % 2][:, b, :], resid[:, b, n * N:(n + 1) * N],
                                                   pbuf[:, n * N:(n + 1) * N], MUL)
                last.then_inc(x_scaled, 1)

            def mean_squares_x():
                dve.wait_ge(x_squared, GROUPS)
                nc.vector.tensor_reduce(ms_x[:, :], ss_x[:, :, :], AX.X, ADD).then_inc(ssx_done, 1)
                dve.wait_ge(ssx_done, 1)
                nc.vector.tensor_scalar(ms_x[:, :], ms_x[:, :], 1.0 / D, EPS, MUL, ADD).then_inc(msx_done, 1)

            def extend_rel_rows():
                dve.wait_ge(rel_in, 16)
                nc.vector.tensor_copy(rel_rows[:, REL:EXT],
                                      rel_rows[:, REL - 1:REL].to_broadcast([D // HD, EXT - REL])) \
                    .then_inc(rel_rows_done, 1)

            def prepare_gains():
                dve.wait_ge(small_in, 16 * 10)
                for i in range(2):
                    nc.vector.scalar_tensor_tensor(out=kq_gain[:, i:i + 1], in0=gains[:, 2 * i:2 * i + 1],
                                                   scalar=SCALE, in1=gains[:, 2 * i + 1:2 * i + 2],
                                                   op0=MUL, op1=MUL).then_inc(kq_gain_done, 1)
                dve.wait_ge(x_scaled, GROUPS)
                nc.vector.tensor_scalar(sub_g[:, :, :], sub_g[:, :, :], 1.0 - LAMBDA_INIT, None, MUL) \
                    .then_inc(conv_done, 1)

            def lambda_products():
                for i in range(2):
                    nc.vector.tensor_tensor(lam_v[:, 2 * i, :], lam_v[:, 2 * i, :], lam_v[:, 2 * i + 1, :],
                                            MUL).then_inc(lam_prod, 1)
                dve.wait_ge(lam_prod, 2)
                nc.vector.tensor_reduce(lam2[:, :], lam_v[:, 0:4:2, :], AX.X, ADD).then_inc(lam_sum, 1)

            def negative_lambda():
                dve.wait_ge(lam_exp, 1)
                nc.vector.tensor_tensor(neg_lam[:, :], lam_e[:, 1:2], lam_e[:, 0:1], SUB) \
                    .then_inc(lam_diff, 1)
                dve.wait_ge(lam_diff, 1)
                nc.vector.tensor_scalar(neg_lam[:, :], neg_lam[:, :], LAMBDA_INIT, None, SUB) \
                    .then_inc(lam_done, 1)

            scale_x(0)
            low_weights(0, 0, reuse=False)
            split_low(0, 1, 1, act_in, 0)
            low_weights(0, 1, reuse=False)
            scale_x(1)
            low_weights(0, 2, reuse=False)
            group_chunks(0, range(2))
            dve.wait_ge(lam_done, 1)
            dve.wait_ge(conv_done, 1)
            dve.wait_ge(mask_ready, 1)
            with dve.Fori(0, GROUPS - 1) as i:
                group_chunks(i, range(2, NC))
                group_chunks(i + 1, range(2))
            group_chunks(GROUPS - 1, range(2, NC))

            def add_residual(chunk, parity, n):
                result_of(chunk)
                cols = slice(n * N, (n + 1) * N)
                nc.vector.tensor_tensor(resid[:, :, cols], acc[parity][:, :, :], resid[:, :, cols], ADD) \
                    .then_inc(acc_read[parity], 1)

            def scale_x1(n):
                dve.wait_ge(acc_read[n % 2], read_no(WO0 + n))
                if n > 0:
                    dve.wait_ge(side_full[0], H2_SIDE + n)
                for b in range(NB):
                    last = nc.vector.tensor_tensor(gbuf[:, b, :], resid[:, b, n * N:(n + 1) * N],
                                                   pbuf[:, n * N:(n + 1) * N], MUL)
                last.then_inc(x1_scaled, 1)

            HI0 = 2 * GROUPS
            for n in range(GROUPS):
                for s in range(STEPS):
                    low_weights(WO0 + n, s + AHEAD)
                    if n == 0:
                        if s == 0:
                            dve.wait_ge(mixb_done, GROUPS)
                            gate_sum(GROUPS - 1, G_C, 2)
                        elif s == 3:
                            add_c(GROUPS - 1)
                        elif s == 5:
                            split_low(0, side_no(0, GROUPS - 1, "mixT"), HI0, act_mid, GROUPS - 1)
                    elif s == 0:
                        add_residual(WO0 + n - 1, (n - 1) % 2, n - 1)
                    elif s == 1:
                        if n == 1:
                            dve.wait_ge(gain2_in, 16)
                        scale_x1(n - 1)
                    elif s == 4:
                        split_low(0, H2_SIDE + n, HI0 + n, act_in, n - 1)

            def quarter_chunks(f, chunks, last_quarter=False):
                first = isinstance(f, int) and f == 0
                for j in chunks:
                    for s in range(STEPS):
                        if not (last_quarter and j == MC - 1 and s + AHEAD >= STEPS):
                            low_weights(f * MC + (MLP0 + j), s + AHEAD)
                        if first and j == 0:
                            if s == 0:
                                add_residual(MLP0 - 1, 1, GROUPS - 1)
                            elif s == 1:
                                scale_x1(GROUPS - 1)
                            elif s == 3:
                                dve.wait_ge(x1_squared, GROUPS)
                                nc.vector.tensor_reduce(ms_h[:, :], ss_h[:, :, :], AX.X, ADD) \
                                    .then_inc(ssh_done, 1)
                                dve.wait_ge(ssh_done, 1)
                                nc.vector.tensor_scalar(ms_h[:, :], ms_h[:, :], 1.0 / D, EPS, MUL, ADD) \
                                    .then_inc(msh_done, 1)
                            elif s == 4:
                                split_low(0, H2_SIDE + GROUPS, HI0 + GROUPS, act_in, GROUPS - 1)
                        elif j == 0 and s == 0:
                            add_residual(f * MC + (MLP0 - 1), 1, GROUPS - 1)
                        if 1 <= j <= GROUPS and s == 4:
                            dve.wait_ge(act_hi, f * GROUPS + (HI0 + GROUPS + j))
                            tiles = slice((j - 1) * KT4, j * KT4)
                            nc.vector.tensor_tensor(
                                act_mid[:, 1, tiles, :],
                                kbuf[:, :, :].rearrange("p b (t k) -> p (b t) k", k=T),
                                act_mid[:, 0, tiles, :].bitcast(F32), SUB).then_inc(side_read[0], 1)
                        if j > GROUPS and s == 0:
                            add_residual(f * MC + (MLP0 + j - 1), (j - 1) % 2, j - 1 - GROUPS)

            quarter_chunks(0, [0])
            with dve.Fori(0, QUARTERS - 1) as i:
                quarter_chunks(i, range(1, MC))
                quarter_chunks(i + 1, [0])
            quarter_chunks(QUARTERS - 1, range(1, MC), last_quarter=True)
            add_residual(MLP0 + QUARTERS * MC - 1, 1, GROUPS - 1)

        @block.gpsimd
        def _(pool):
            nc.gpsimd.memset(ident[:, :], 0.0).then_inc(ident_set, 1)
            nc.gpsimd.memset(mask[:, :], 0.0).then_inc(mask_set, 1)
            pool.wait_ge(ident_set, 1)
            nc.gpsimd.affine_select(out=ident[:, :], in_=ident[:, :], compare_op=ALU.not_equal, fill=1.0,
                                    base=0, pattern=[[-1, P]], channel_multiplier=1) \
                .then_inc(ident_ready, 1)
            pool.wait_ge(mask_set, 1)
            nc.gpsimd.memset(mask[0:CHUNK, T - CHUNK:T], NEG).then_inc(mask_ready, 1)
            nc.gpsimd.memset(neg_half[:, :], -0.5).then_inc(half_ready, 1)
            pool.wait_ge(half_ready, 1)

            def rsqrt(dst, src, n):
                return nc.gpsimd.tensor_tensor(dst, src, neg_half[:, 0:n], ALU.pow)

            pool.dma_start(rel_rows[:, 0:REL], a_rel_bias[0]).then_inc(rel_in, 16)
            for i, v in enumerate((a_qn_g, a_kn_g, b_qn_g, b_kn_g)):
                pool.dma_start(gains[:, i:i + 1], v[0, :].rearrange("(d o) -> d o", o=1)) \
                    .then_inc(small_in, 16)
            for i, v in enumerate((b_lq1, b_lk1, b_lq2, b_lk2)):
                pool.dma_start(lam_v[:, i, :], v[0, :].partition_broadcast(P)).then_inc(small_in, 16)
            for i in range(2):
                pool.dma_start(sub_g[:, i, :], b_subln_g[0, :].partition_broadcast(P)) \
                    .then_inc(small_in, 16)
            pool.wait_ge(rel_rows_done, 1)
            pool.dma_start(rel_ext.ap(), rel_rows[:, :]).then_inc(rel_stored, 16)
            pool.wait_ge(msx_done, 1)
            rsqrt(r_x[:, :], ms_x[:, :], NB).then_inc(rx_done, 1)

            def square(g, c, src, e):
                pool.wait_ge(acc_read[c % 2], acc_no(g, NC, c))
                nc.gpsimd.tensor_tensor(scratch2, src[:, :, :], src[:, :, :], MUL).then_inc(sq_done, 1)

            def rms(g, dst, e):
                pool.wait_ge(ms_done, g * 4 + (e + 1))
                rsqrt(dst[:, :], meansq[:, :], 8).then_inc(rstd_done, 1)

            def normalise_keys(g, e, i):
                pool.wait_ge(rstd_done, g * 4 + (e + 1))
                k3 = kbuf[:, :, :].rearrange("p b (m d) -> p (b m) d", d=HD)
                nc.gpsimd.tensor_tensor(k3, k3, r_k[:, :].unsqueeze(2).to_broadcast([P, 8, HD]), MUL) \
                    .then_inc(kn_done, 1)

            def mask_bias(g):
                pool.wait_ge(rel_loaded, g * 16 + 16)
                masked = rel[0:CHUNK, :, 0:CHUNK]
                neg = mask[0:CHUNK, T - CHUNK:T].unsqueeze(1).to_broadcast([CHUNK, MAPS, CHUNK])
                nc.gpsimd.tensor_tensor(masked, masked, neg, ADD).then_inc(rel_ready, 1)

            def add_b(g):
                pool.wait_ge(side_read[1], side_no(1, g, "out_b"))
                pool.wait_ge(gate_done, g * 3 + 2)
                nc.gpsimd.tensor_tensor(scratch2, scratch2, gbuf[:, :, :], MUL).then_inc(outb_gated, 1)
                pool.wait_ge(outb_gated, g + 1)
                nc.gpsimd.tensor_tensor(mix[:, :, :], mix[:, :, :], scratch2, ADD).then_inc(mixb_done, 1)

            def convolve(g):
                pool.wait_ge(shifted, g * 64 + 64)
                pool.wait_ge(taps_in, g * 16 + 16)
                for tap, t in ((0, u2), (1, u1), (2, kbuf)):
                    for b in range(NB):
                        nc.gpsimd.tensor_tensor(t[:, b, :], t[:, b, :], conv_w[:, tap, :], MUL) \
                            .then_inc(taps_done, 1)
                pool.wait_ge(taps_done, g * 6 + 6)
                nc.gpsimd.tensor_tensor(u1, u1, u2, ADD).then_inc(tap_sum, 1)
                pool.wait_ge(tap_sum, g + 1)
                nc.gpsimd.tensor_tensor(kbuf[:, :, :], kbuf[:, :, :], u1, ADD).then_inc(conv_done, 1)

            def group(g):
                square(g, K_A, kbuf, 0)
                rms(g, r_k, 0)
                normalise_keys(g, 0, 0)
                mask_bias(g)
                square(g, Q_A, qbuf, 1)
                rms(g, r_q, 1)
                square(g, K_B, kbuf, 2)
                rms(g, r_k, 2)
                normalise_keys(g, 2, 1)
                square(g, Q_B, qbuf, 3)
                rms(g, r_q, 3)
                pool.wait_ge(ssb_done, g + 1)
                pool.wait_ge(msb_done, g + 1)
                rsqrt(r_b[:, :], ms_b[:, :], 4).then_inc(rstdb_done, 1)
                nc.gpsimd.memset(pbuf[0:2, 0:N], 0.0)
                nc.gpsimd.memset(pbuf[0:2, NB * N:NB * N + N], 0.0).then_inc(zero_rows, 1)
                add_b(g)
                convolve(g)

            with pool.Fori(0, GROUPS) as g:
                group(g)
            pool.wait_ge(msh_done, 1)
            rsqrt(r_h[:, :], ms_h[:, :], NB).then_inc(rh_done, 1)


_INS = ["x", "norm1_g", "w_in", "w_gate", "b_gate", "a_qn_g", "a_kn_g", "a_rel_bias", "b_qn_g", "b_kn_g",
        "b_lq1", "b_lk1", "b_lq2", "b_lk2", "b_subln_g", "c_conv_w", "w_o", "norm2_g", "w_mlp1", "w_mlp2"]


def kernel(**inputs):
    import numpy as _np
    import concourse.bacc as _bacc
    from concourse import mybir as _mybir
    from concourse.bass_utils import run_bass_kernel_spmd as _run

    nc = _bacc.Bacc("TRN2", target_bir_lowering=False, num_devices=1)
    arrays, args = {}, []
    for name in _INS:
        a = _np.ascontiguousarray(inputs[name])
        arrays[f"in_{name}_dram"] = a
        args.append(nc.dram_tensor(f"in_{name}_dram", a.shape, _mybir.dt.from_np(a.dtype),
                                   kind="ExternalInput").ap())
    shape = arrays["in_x_dram"].shape
    args.append(nc.dram_tensor("out_dram", shape, _mybir.dt.float32, kind="ExternalOutput").ap())
    build_trunk(nc, *args)
    r = _run(nc, [arrays], core_ids=[0])
    return r.results[0]["out_dram"]
```

```python
import math
from contextlib import ExitStack

import concourse.bass as bass
from concourse import mybir


def build_trunk(nc, x, norm1_g, w_in, w_gate, b_gate, a_qn_g, a_kn_g, a_rel_bias, b_qn_g, b_kn_g,
                b_lq1, b_lk1, b_lq2, b_lk2, b_subln_g, c_conv_w, w_o, norm2_g, w_mlp1, w_mlp2, out):
    F32, F32R = mybir.dt.float32, mybir.dt.float32r
    ALU, ACT, AX = mybir.AluOpType, mybir.ActivationFunctionType, mybir.AxisListType
    MUL, ADD, SUB = ALU.mult, ALU.add, ALU.subtract

    P = 128
    D = x.shape[2]
    NB = x.shape[1] // P
    T = NB * P
    N = 512
    KT = D // P
    STEPS = KT // 2
    HD = 128
    GROUPS = D // N
    NC = 12
    MAPS = N // HD
    KT4 = N // P
    CHUNK = 64
    MAX_REL = 128
    REL = a_rel_bias.shape[2]
    EXT = 384
    EPS = 1e-6
    SCALE = HD ** -0.5
    LAMBDA_INIT = 0.8 - 0.6 * math.exp(-0.3 * 0)
    NEG = -1.0e30
    RAW, RING = 4, 4
    AHEAD = RING - 1
    QUARTERS = w_mlp1.shape[2] // D
    WO0 = GROUPS * NC
    MLP0 = WO0 + GROUPS
    MC = 2 * GROUPS

    K_A, Q_A, V_A, G_A, K_B, Q_B, V_B, G_B, C_G, X_C, B_G, G_C = range(NC)
    PARTS = {K_A: (w_in, D), Q_A: (w_in, 0), V_A: (w_in, 2 * D), G_A: (w_gate, 0),
             K_B: (w_in, 4 * D), Q_B: (w_in, 3 * D), V_B: (w_in, 5 * D), G_B: (w_gate, D),
             C_G: (w_in, 7 * D), X_C: (w_in, 8 * D), B_G: (w_in, 6 * D), G_C: (w_gate, 2 * D)}

    def by_ktile(w):
        return w[0].rearrange("(k p) n -> p k n", p=P)

    ctx = ExitStack()
    with ctx:
        def sb(name, shape, dt=F32):
            return ctx.enter_context(nc.sbuf_tensor(name, shape, dt))

        def sem(name):
            return ctx.enter_context(nc.semaphore(name))

        act_in = sb("act_in", [P, 2, KT, T], F32R)
        act_mid = sb("act_mid", [P, 2, KT, T], F32R)
        raw = sb("raw", [P, RAW, 4, N])
        w_hi = sb("w_hi", [P, RING, 2, N], F32R)
        w_lo = sb("w_lo", [P, RING, 2, N], F32R)
        resid = sb("resid", [P, NB, D])
        kbuf = sb("kbuf", [P, NB, N])
        qbuf = sb("qbuf", [P, NB, N])
        vbuf = sb("vbuf", [P, NB, N])
        gbuf = sb("gbuf", [P, NB, N])
        mix = sb("mix", [P, NB, N])
        kT = act_mid[:, :, KT - MAPS:KT, :]
        qT = sb("qT", [P, 2, MAPS, P], F32R)
        kT0 = sb("kT0", [P, MAPS, P])
        qT0 = sb("qT0", [P, MAPS, P])
        sbuf_s = sb("scores", [P, MAPS * 3 * P])
        pbuf = sb("pbuf", [P, 4 * N])
        rel = sb("rel", [P, MAPS, 2 * P])
        conv_w = sb("conv_w", [P, 3, N])
        gate_b = sb("gate_b", [P, 3, N])
        sub_g = sb("sub_g", [P, 2, 2 * HD])
        mask = sb("mask", [P, 2 * P])
        ident = sb("ident", [P, P])
        norm_rows = pbuf[0:2 * KT, 0:P]
        norm_g = sb("norm_g", [P, 2, KT])
        rel_rows = gbuf[0:D // HD, 0, 0:EXT]
        gains = sb("gains", [P, 4])
        kq_gain = sb("kq_gain", [P, 2])
        neg_half = sb("neg_half", [P, 8])
        lam_v = vbuf[:, 0, :].rearrange("p (v d) -> p v d", v=4)
        lam2 = sb("lam2", [P, 2])
        lam_e = sb("lam_e", [P, 2])
        neg_lam = sb("neg_lam", [P, 1])
        ss_x = sb("ss_x", [P, NB, 4])
        ss_h = sb("ss_h", [P, NB, 4])
        ms_x = sb("ms_x", [P, NB])
        r_x = sb("r_x", [P, NB])
        ms_h = sb("ms_h", [P, NB])
        r_h = sb("r_h", [P, NB])
        sumsq = sb("sumsq", [P, 8])
        meansq = sb("meansq", [P, 8])
        r_k = sb("r_k", [P, 8])
        r_q = sb("r_q", [P, 8])
        neg_max = sb("neg_max", [P, 8])
        row_sum = sb("row_sum", [P, 8])
        r_sum = sb("r_sum", [P, 8])
        lam_ratio = sb("lam_ratio", [P, 4])
        ss_b = sb("ss_b", [P, 4])
        ms_b = sb("ms_b", [P, 4])
        r_b = sb("r_b", [P, 4])
        coef_b = sb("coef_b", [P, 4])
        rel_ext = nc.dram_tensor("rel_ext", (D // HD, EXT), F32, kind="Internal")

        acc = [ctx.enter_context(nc.psum_tensor(f"acc{p}", [P, NB, N], F32)) for p in range(2)]
        side = [ctx.enter_context(nc.psum_tensor(f"side{p}", [P, 2 * N], F32)) for p in range(2)]

        s3 = sbuf_s[:, :].rearrange("p (m k) -> p m k", m=MAPS)
        scratch = sbuf_s[:, 0:NB * N]
        scratch2 = scratch.rearrange("p (b n) -> p b n", b=NB)
        pT = pbuf[:, 0:12 * P].rearrange("p (t k) -> p t k", t=12)
        u1 = pbuf[:, 0:NB * N].rearrange("p (b n) -> p b n", b=NB)
        u2 = pbuf[:, NB * N:2 * NB * N].rearrange("p (b n) -> p b n", b=NB)

        raw_full = [sem(f"raw_full{q}") for q in range(RAW)]
        hi_ready = sem("hi_ready")
        lo_ready = sem("lo_ready")
        step_done = sem("step_done")
        acc_read = [sem(f"acc_read{p}") for p in range(2)]
        side_full = [sem(f"side_full{p}") for p in range(2)]
        side_read = [sem(f"side_read{p}") for p in range(2)]
        act_hi = sem("act_hi")
        first_raw = sem("first_raw")
        first_x = sem("first_x")
        first_turned = sem("first_turned")
        first_hi = sem("first_hi")
        first_lo = sem("first_lo")
        x_in = [sem(f"x_in{n}") for n in range(GROUPS)]
        norm_in = sem("norm_in")
        norm_turned = sem("norm_turned")
        norm_ready = sem("norm_ready")
        small_in = sem("small_in")
        rel_in = sem("rel_in")
        rel_rows_done = sem("rel_rows_done")
        rel_stored = sem("rel_stored")
        rel_loaded = sem("rel_loaded")
        rel_ready = sem("rel_ready")
        taps_in = sem("taps_in")
        gateb_in = sem("gateb_in")
        ident_set = sem("ident_set")
        ident_ready = sem("ident_ready")
        mask_set = sem("mask_set")
        mask_ready = sem("mask_ready")
        half_ready = sem("half_ready")
        x_squared = sem("x_squared")
        ssx_done = sem("ssx_done")
        msx_done = sem("msx_done")
        rx_done = sem("rx_done")
        kq_gain_done = sem("kq_gain_done")
        lam_prod = sem("lam_prod")
        lam_sum = sem("lam_sum")
        lam_exp = sem("lam_exp")
        lam_diff = sem("lam_diff")
        lam_done = sem("lam_done")
        sq_done = sem("sq_done")
        ss_done = sem("ss_done")
        ms_done = sem("ms_done")
        rstd_done = sem("rstd_done")
        kn_done = sem("kn_done")
        k_hi = sem("k_hi")
        q_hi = sem("q_hi")
        max_done = sem("max_done")
        exp_done = sem("exp_done")
        rsum_done = sem("rsum_done")
        ratio_done = sem("ratio_done")
        comb_done = sem("comb_done")
        gate_done = sem("gate_done")
        ssb_done = sem("ssb_done")
        msb_done = sem("msb_done")
        rstdb_done = sem("rstdb_done")
        coefb_done = sem("coefb_done")
        outb_done = sem("outb_done")
        outb_gated = sem("outb_gated")
        mixb_done = sem("mixb_done")
        zero_rows = sem("zero_rows")
        shifted = sem("shifted")
        taps_done = sem("taps_done")
        tap_sum = sem("tap_sum")
        conv_done = sem("conv_done")
        gated_c = sem("gated_c")
        mix_done = sem("mix_done")
        x1_squared = sem("x1_squared")
        ssh_done = sem("ssh_done")
        msh_done = sem("msh_done")
        rh_done = sem("rh_done")
        hid_squared = sem("hid_squared")
        block_done = sem("block_done")
        block_summed = sem("block_summed")
        stored = sem("stored")

        def chunk_of(g, c):
            return g * NC + c

        SIDE = [["kT_a", "scores_a", "pT_a", "kT_b", "scores_b", "pT_b", "mixT"],
                ["qT_a", "scores_a", "pT_a", "out_a", "qT_b", "scores_b", "out_b"]]
        FIRST_SIDE = GROUPS // 2

        def side_no(p, g, name):
            return g * len(SIDE[p]) + (FIRST_SIDE + SIDE[p].index(name) + 1)

        H2_SIDE = FIRST_SIDE + GROUPS * len(SIDE[0])
        HID_SIDE = H2_SIDE + GROUPS

        def acc_no(chunk_g, per, c):
            return chunk_g * (per // 2) + (c // 2 + 1)

        def read_no(chunk):
            return chunk // 2 + 1

        def ab(c):
            return 0 if c < K_B else 1

        block = ctx.enter_context(nc.Block())

        @block.sync
        def _(sp):
            def column(g, col=0):
                return g * N + col if isinstance(g, int) else (g + 1) * N + (col - N)

            def load_weights(w, chunk, n0):
                for q in range(RAW):
                    sp.wait_ge(lo_ready, (chunk - 1) * STEPS + 2 * q + 2)
                    sp.dma_start(raw[:, q, :, :], by_ktile(w)[:, 4 * q:4 * q + 4, bass.ds(n0, N)]) \
                        .then_inc(raw_full[q], 16)

            def load_down(w, chunk, f, n):
                wk = w[0].rearrange("(k p) n -> p k n", p=P)
                for q in range(RAW):
                    sp.wait_ge(lo_ready, (chunk - 1) * STEPS + 2 * q + 2)
                    sp.dma_start(raw[:, q, :, :], wk[:, bass.ds(f * KT + 4 * q, 4), n * N:(n + 1) * N]) \
                        .then_inc(raw_full[q], 16)

            def load_group_constants(g):
                first = isinstance(g, int) and g == 0
                if first:
                    sp.wait_ge(rel_stored, 16)
                else:
                    sp.wait_ge(side_read[1], side_no(1, g - 1, "scores_a"))
                sp.dma_start(rel[:, :, :], bass.AP(rel_ext, g * (MAPS * EXT) + 1,
                                                   [[1, P], [EXT, MAPS], [1, 2 * P]])) \
                    .then_inc(rel_loaded, 16)
                if not first:
                    sp.wait_ge(conv_done, g + 1)
                taps = c_conv_w[0, :, bass.ds(column(g), N)]
                sp.dma_start(conv_w[:, :, :], taps.partition_broadcast(P)).then_inc(taps_in, 16)
                if not first:
                    sp.wait_ge(gate_done, g * 3)
                bias = b_gate[0, :].rearrange("(j n) -> j n", j=3)[:, bass.ds(column(g), N)]
                sp.dma_start(gate_b[:, :, :], bias.partition_broadcast(P)).then_inc(gateb_in, 16)

            def group_chunks(g, chunks):
                for c in chunks:
                    if c == 1 and not (isinstance(g, int) and g == 0):
                        load_group_constants(g)
                    w, col = PARTS[c]
                    load_weights(w, chunk_of(g, c), column(g, col))

            xr = x[0].rearrange("(b p) d -> p b d", p=P)
            w, col = PARTS[0]
            sp.dma_start(resid[:, :, 0:2 * P], xr[:, :, 0:2 * P]).then_inc(first_x, 16)
            sp.dma_start(raw[:, 0, 0:2, :], by_ktile(w)[:, 0:2, col:col + N]).then_inc(first_raw, 16)
            sp.dma_start(resid[:, :, 2 * P:N], xr[:, :, 2 * P:N]).then_inc(x_in[0], 16)
            sp.dma_start(raw[:, 0, 2:4, :], by_ktile(w)[:, 2:4, col:col + N]).then_inc(raw_full[0], 16)
            for n in range(1, GROUPS):
                cols = slice(n * N, (n + 1) * N)
                sp.dma_start(resid[:, :, cols], xr[:, :, cols]).then_inc(x_in[n], 16)
                sp.dma_start(raw[:, n, :, :], by_ktile(w)[:, 4 * n:4 * n + 4, col:col + N]) \
                    .then_inc(raw_full[n], 16)
            group_chunks(0, [1])
            load_group_constants(0)
            with sp.Fori(0, GROUPS - 1) as i:
                group_chunks(i, range(2, NC))
                group_chunks(i + 1, range(2))
            group_chunks(GROUPS - 1, range(2, NC))
            for n in range(GROUPS):
                load_weights(w_o, WO0 + n, n * N)

            def quarter(f):
                for j in range(GROUPS):
                    load_weights(w_mlp1, f * MC + (MLP0 + j), f * D + j * N)
                for n in range(GROUPS):
                    load_down(w_mlp2, f * MC + (MLP0 + GROUPS + n), f, n)

            with sp.Fori(0, QUARTERS) as f:
                quarter(f)
            outr = out[0].rearrange("(b p) d -> p b d", p=P)
            for n in range(GROUPS - 1):
                last = MLP0 + QUARTERS * MC - GROUPS + n
                sp.wait_ge(acc_read[last % 2], read_no(last))
                sp.dma_start(outr[:, :, n * N:(n + 1) * N], resid[:, :, n * N:(n + 1) * N]) \
                    .then_inc(stored, 16)
            for b in range(NB):
                sp.wait_ge(block_summed, b + 1)
                sp.dma_start(outr[:, b, D - N:D], resid[:, b, D - N:D]).then_inc(stored, 16)
            sp.wait_ge(stored, 16 * (GROUPS - 1 + NB))

        @block.tensor
        def _(pe):
            def product(o, left, right, start=True, stop=True):
                nc.tensor.matmul(o, left[0], right[0], start=start, stop=False)
                nc.tensor.matmul(o, left[0], right[1], start=False, stop=False)
                return nc.tensor.matmul(o, left[1], right[0], start=False, stop=stop)

            def transpose_tile(pair, src):
                for t in range(KT4):
                    for b in range(NB):
                        last = nc.tensor.transpose(side[pair][:, t * T + b * P:t * T + (b + 1) * P],
                                                   src[:, b, t * P:(t + 1) * P], ident[:, :])
                return last

            def step(chunk, parity, s, act, very_last=False):
                pe.wait_ge(lo_ready, chunk * STEPS + (s + 1))
                for b in range(NB):
                    for kk in range(2):
                        k = 2 * s + kk
                        last = product(acc[parity][:, b, :],
                                       [act[:, part, k, b * P:(b + 1) * P] for part in range(2)],
                                       [w[:, s % RING, kk, :] for w in (w_hi, w_lo)],
                                       start=(k == 0), stop=(k == KT - 1))
                    if b == 0 and very_last:
                        last.then_inc(block_done, 1)
                last.then_inc(step_done, 1)

            def free_acc(g, per, c):
                pe.wait_ge(acc_read[c % 2], acc_no(g, per, c) - 1)

            def start_side(pair, no):
                pe.wait_ge(side_read[pair], no - 1)

            def transpose_keys(g, c):
                no = side_no(0, g, "kT_a" if c == K_A else "kT_b")
                start_side(0, no)
                pe.wait_ge(kn_done, g * 2 + (ab(c) + 1))
                for m in range(MAPS):
                    for b in range(NB):
                        last = nc.tensor.transpose(side[0][:, m * T + b * P:m * T + (b + 1) * P],
                                                   kbuf[:, b, m * HD:(m + 1) * HD], ident[:, :])
                last.then_inc(side_full[0], 1)

            def transpose_queries(g, c):
                no = side_no(1, g, "qT_a" if c == Q_A else "qT_b")
                start_side(1, no)
                pe.wait_ge(acc_read[c % 2], acc_no(g, NC, c))
                for m in range(MAPS):
                    for b in range(NB):
                        last = nc.tensor.transpose(side[1][:, m * T + b * P:m * T + (b + 1) * P],
                                                   qbuf[:, b, m * HD:(m + 1) * HD], ident[:, :])
                last.then_inc(side_full[1], 1)

            def scores(g, br):
                name = "scores_" + br
                pe.wait_ge(side_read[0], side_no(0, g, "kT_" + br))
                pe.wait_ge(side_read[1], side_no(1, g, "qT_" + br))
                for m in range(MAPS):
                    last = product(side[0][:, m * T:(m + 1) * T], [qT[:, part, m, :] for part in range(2)],
                                   [kT[:, part, m, :] for part in range(2)])
                last.then_inc(side_full[0], 1)
                for m in range(MAPS):
                    last = nc.tensor.matmul(side[1][:, m * P:(m + 1) * P], qT0[:, m, :], kT0[:, m, :],
                                            start=True, stop=True)
                last.then_inc(side_full[1], 1)

            def transpose_probs_a(g):
                start_side(1, side_no(1, g, "pT_a"))
                start_side(0, side_no(0, g, "pT_a"))
                pe.wait_ge(exp_done, g * 2 + 1)
                for t in list(range(8, 12)) + list(range(8)):
                    m, part = t // 3, t % 3
                    o = side[t // 8][:, (t % 8) * P:(t % 8 + 1) * P]
                    last = nc.tensor.transpose(o, s3[:, m, part * P:(part + 1) * P], ident[:, :])
                    if t == 11:
                        last.then_inc(side_full[1], 1)
                last.then_inc(side_full[0], 1)

            def transpose_probs_b(g):
                start_side(0, side_no(0, g, "pT_b"))
                pe.wait_ge(comb_done, g + 1)
                for t in range(6):
                    m, part = 2 * (t // 3), t % 3
                    last = nc.tensor.transpose(side[0][:, t * P:(t + 1) * P],
                                               s3[:, m, part * P:(part + 1) * P], ident[:, :])
                last.then_inc(side_full[0], 1)

            def values(g, br, heads, width):
                start_side(1, side_no(1, g, "out_" + br))
                pe.wait_ge(side_read[0], side_no(0, g, "pT_" + br))
                c = V_A if br == "a" else V_B
                pe.wait_ge(acc_read[c % 2], acc_no(g, NC, c))
                for h in range(heads):
                    cols = slice(h * width, (h + 1) * width)
                    nc.tensor.matmul(side[1][:, cols], pT[:, 3 * h + 2, :], vbuf[:, 0, cols],
                                     start=True, stop=True)
                    o = side[1][:, N + h * width:N + (h + 1) * width]
                    nc.tensor.matmul(o, pT[:, 3 * h, :], vbuf[:, 0, cols], start=True, stop=False)
                    last = nc.tensor.matmul(o, pT[:, 3 * h + 1, :], vbuf[:, 1, cols],
                                            start=False, stop=True)
                last.then_inc(side_full[1], 1)

            def transpose_mix(g):
                start_side(0, side_no(0, g, "mixT"))
                pe.wait_ge(mix_done, g + 1)
                transpose_tile(0, mix).then_inc(side_full[0], 1)

            def group_chunks(g, chunks):
                first = isinstance(g, int) and g == 0
                for c in chunks:
                    for s in range(STEPS):
                        if s == 0 and not (first and c < 2):
                            free_acc(g, NC, c)
                        if (c, s) == (0, 5) and not first:
                            transpose_mix(g - 1)
                        elif (c, s) == (1, 5):
                            transpose_keys(g, K_A)
                        elif (c, s) == (2, 2):
                            transpose_queries(g, Q_A)
                        elif (c, s) == (3, 0):
                            scores(g, "a")
                        elif (c, s) == (4, 1):
                            transpose_probs_a(g)
                        elif (c, s) == (4, 5):
                            values(g, "a", MAPS, HD)
                        elif (c, s) == (5, 5):
                            transpose_keys(g, K_B)
                        elif (c, s) == (6, 2):
                            transpose_queries(g, Q_B)
                        elif (c, s) == (7, 0):
                            scores(g, "b")
                        elif (c, s) == (8, 1):
                            transpose_probs_b(g)
                        elif (c, s) == (8, 4):
                            values(g, "b", MAPS // 2, 2 * HD)
                        if first and c == 0:
                            if s == 0:
                                pe.wait_ge(first_lo, 1)
                            elif s == 1:
                                pe.wait_ge(side_read[0], 1)
                            elif s % 2 == 0:
                                pe.wait_ge(side_read[s // 2 % 2], s // 4 + 1)
                            if s in (2, 4):
                                transpose_x(s // 2 + 1)
                        step(chunk_of(g, c), c % 2, s, act_in)

            def transpose_x(n):
                if n >= 2:
                    start_side(n % 2, n // 2 + 1)
                pe.wait_ge(x_in[n], 16)
                transpose_tile(n % 2, resid[:, :, n * N:(n + 1) * N]).then_inc(side_full[n % 2], 1)

            def transpose_two(k):
                for t in (k, k + 1):
                    for b in range(NB):
                        last = nc.tensor.transpose(side[0][:, t * T + b * P:t * T + (b + 1) * P],
                                                   resid[:, b, t * P:(t + 1) * P], ident[:, :])
                return last

            pe.wait_ge(ident_ready, 1)
            pe.wait_ge(norm_in, 32)
            nc.tensor.transpose(acc[1][:, 0, 0:2 * KT], norm_rows, ident[0:2 * KT, 0:2 * KT]) \
                .then_inc(norm_turned, 1)
            pe.wait_ge(first_x, 16)
            transpose_two(0).then_inc(first_turned, 1)
            pe.wait_ge(x_in[0], 16)
            transpose_two(2).then_inc(side_full[0], 1)
            transpose_x(1)
            group_chunks(0, [0])
            pe.wait_ge(norm_ready, 1)
            group_chunks(0, [1])
            with pe.Fori(0, GROUPS - 1) as i:
                group_chunks(i, range(2, NC))
                group_chunks(i + 1, range(2))
            group_chunks(GROUPS - 1, range(2, NC))

            def transpose_h2(n):
                start_side(0, H2_SIDE + n + 1)
                pe.wait_ge(acc_read[n % 2], read_no(WO0 + n))
                transpose_tile(0, resid[:, :, n * N:(n + 1) * N]).then_inc(side_full[0], 1)

            for n in range(GROUPS):
                for s in range(STEPS):
                    if s == 0:
                        free_acc(0, 2, WO0 + n)
                        if n == 0:
                            pe.wait_ge(side_read[0], side_no(0, GROUPS - 2, "mixT"))
                    if (n, s) == (0, 5):
                        transpose_mix(GROUPS - 1)
                    if (n, s) == (0, 6):
                        pe.wait_ge(side_read[0], side_no(0, GROUPS - 1, "mixT"))
                    if n > 0 and s == 3:
                        transpose_h2(n - 1)
                    step(WO0 + n, n % 2, s, act_mid)

            def transpose_hidden(f, j):
                start_side(0, f * GROUPS + (HID_SIDE + j + 1))
                pe.wait_ge(acc_read[j % 2], f * (MC // 2) + read_no(MLP0 + j))
                transpose_tile(0, qbuf).then_inc(side_full[0], 1)

            def quarter_chunks(f, chunks, last_quarter=False):
                first = isinstance(f, int) and f == 0
                for j in chunks:
                    for s in range(STEPS):
                        if s == 0:
                            pe.wait_ge(acc_read[j % 2], f * (MC // 2) + (MLP0 + j) // 2)
                        if first and j == 0:
                            if s == 0:
                                pe.wait_ge(side_read[0], H2_SIDE + GROUPS - 1)
                            elif s == 3:
                                transpose_h2(GROUPS - 1)
                            elif s == 6:
                                pe.wait_ge(side_read[0], H2_SIDE + GROUPS)
                        if 1 <= j <= GROUPS and s == 2:
                            transpose_hidden(f, j - 1)
                        if j == GROUPS and s == 0:
                            pe.wait_ge(side_read[0], f * GROUPS + (HID_SIDE + GROUPS - 1))
                        if j == GROUPS and s == 6:
                            pe.wait_ge(side_read[0], f * GROUPS + (HID_SIDE + GROUPS))
                        step(f * MC + (MLP0 + j), j % 2, s, act_in if j < GROUPS else act_mid,
                             very_last=last_quarter and (j, s) == (MC - 1, STEPS - 1))

            quarter_chunks(0, [0])
            with pe.Fori(0, QUARTERS - 1) as i:
                quarter_chunks(i, range(1, MC))
                quarter_chunks(i + 1, [0])
            quarter_chunks(QUARTERS - 1, range(1, MC), last_quarter=True)

        @block.scalar
        def _(act):
            def round_weights(chunk, i, reuse=True):
                q, half = i % STEPS // 2, i % 2
                if reuse or i > 0:
                    act.wait_ge(raw_full[q], (chunk + i // STEPS) * 16 + 16)
                else:
                    act.wait_ge(first_raw, 16)
                if reuse:
                    act.wait_ge(step_done, chunk * STEPS + (i - RING + 1))
                nc.scalar.activation(w_hi[:, i % RING, :, :], raw[:, q, 2 * half:2 * half + 2, :],
                                     ACT.Copy).then_inc(hi_ready, 1)

            def result_of(chunk):
                act.wait_ge(step_done, chunk * STEPS + STEPS)

            def evacuate(g, c, dst):
                result_of(chunk_of(g, c))
                nc.scalar.activation(dst[:, 0, :], acc[c % 2][:, 0, :], ACT.Copy, scale=r_x[:, 0:1])
                nc.scalar.activation(dst[:, 1, :], acc[c % 2][:, 1, :], ACT.Copy, scale=r_x[:, 1:2]) \
                    .then_inc(acc_read[c % 2], 1)

            def keys_out(g, br):
                act.wait_ge(side_full[0], side_no(0, g, "kT_" + br))
                i = "ab".index(br)
                keys = side[0][:, :].rearrange("p (m t) -> p m t", m=MAPS)
                nc.scalar.activation(kT0[:, :, :], keys[:, :, 0:P], ACT.Copy, scale=kq_gain[:, i:i + 1])
                nc.scalar.activation(kT[:, 0, :, :], keys, ACT.Copy, scale=kq_gain[:, i:i + 1]) \
                    .then_inc(k_hi, 1)

            def queries_out(g, br):
                act.wait_ge(side_full[1], side_no(1, g, "qT_" + br))
                queries = side[1][:, :].rearrange("p (m t) -> p m t", m=MAPS)
                nc.scalar.activation(qT[:, 0, :, :], queries[:, :, P:T], ACT.Copy).then_inc(q_hi, 1)

            def exponentials(g, br, b):
                if b == 1:
                    act.wait_ge(max_done, g * 2 + ("ab".index(br) + 1))
                cols = slice(0, T) if b == 1 else slice(T, T + P)
                for m in range(MAPS):
                    i = b * MAPS + m
                    last = nc.scalar.activation(s3[:, m, cols], s3[:, m, cols], ACT.Exp,
                                                bias=neg_max[:, i:i + 1], accum_out=row_sum[:, i:i + 1])
                if b == 0:
                    last.then_inc(exp_done, 1)

            def gate(g, c):
                act.wait_ge(acc_read[c % 2], acc_no(g, NC, c))
                nc.scalar.activation(gbuf[:, :, :], gbuf[:, :, :], ACT.Sigmoid).then_inc(gate_done, 1)

            def probs_out(g, br, tiles):
                act.wait_ge(side_full[0], side_no(0, g, "pT_" + br))
                nc.scalar.activation(pT[:, 0:tiles, :],
                                     side[0][:, 0:tiles * P].rearrange("p (t k) -> p t k", k=P),
                                     ACT.Copy).then_inc(side_read[0], 1)

            def square_sums_b(g):
                act.wait_ge(side_full[1], side_no(1, g, "out_b"))
                act.wait_ge(rsum_done, g * 2 + 2)
                for b in range(NB):
                    for h in range(2):
                        i = 2 * b + h
                        m = MAPS * b + 2 * h
                        cols = slice(b * N + h * 2 * HD, b * N + (h + 1) * 2 * HD)
                        last = nc.scalar.activation(scratch[:, cols], side[1][:, cols], ACT.Square,
                                                    scale=r_sum[:, m:m + 1],
                                                    accum_out=ss_b[:, i:i + 1])
                last.then_inc(ssb_done, 1)

            def shift_u(g):
                act.wait_ge(acc_read[X_C % 2], acc_no(g, NC, X_C))
                act.wait_ge(zero_rows, g + 1)
                for d, dst in ((1, u1), (2, u2)):
                    act.dma_start(dst[d:P, :, :], kbuf[0:P - d, :, :]).then_inc(shifted, 16)
                    act.dma_start(dst[0:d, 1, :], kbuf[P - d:P, 0, :]).then_inc(shifted, 16)

            def high_scaled(pair, n, norm, tiles=range(KT4)):
                for t in tiles:
                    k = n * KT4 + t
                    last = nc.scalar.activation(act_in[:, 0, k, :], side[pair][:, t * T:(t + 1) * T],
                                                ACT.Copy, scale=norm_g[:, norm, k:k + 1])
                return last

            def split_high_scaled(pair, no, n, norm):
                act.wait_ge(side_full[pair], no)
                high_scaled(pair, n, norm).then_inc(act_hi, 1)

            def split_high(pair, no, dst, n):
                act.wait_ge(side_full[pair], no)
                nc.scalar.activation(dst[:, 0, bass.ds(n * KT4, KT4), :],
                                     side[pair][:, :].rearrange("p (t k) -> p t k", t=KT4),
                                     ACT.Copy).then_inc(act_hi, 1)

            def group_chunks(g, chunks):
                first = isinstance(g, int) and g == 0
                for c in chunks:
                    for s in range(STEPS):
                        round_weights(chunk_of(g, c), s + AHEAD, reuse=not (first and c == 0 and s == 0))
                        if c == 0 and first:
                            if s == 2:
                                split_high_scaled(0, 2, 2, 0)
                            elif s == 4:
                                split_high_scaled(1, 2, 3, 0)
                            if s in (1, 3, 5, 6):
                                x_squares((s - 1) // 2 if s < 6 else 3)
                        if c == 0 and not first:
                            if s == 1:
                                gate(g - 1, G_C)
                            elif s == 5:
                                split_high(0, side_no(0, g - 1, "mixT"), act_mid, g - 1)
                        if (c, s) == (1, 0):
                            evacuate(g, K_A, kbuf)
                        elif (c, s) == (1, 6):
                            keys_out(g, "a")
                        elif (c, s) == (2, 0):
                            evacuate(g, Q_A, qbuf)
                        elif (c, s) == (2, 3):
                            queries_out(g, "a")
                        elif (c, s) == (3, 0):
                            evacuate(g, V_A, vbuf)
                        elif (c, s) == (3, 4):
                            exponentials(g, "a", 1)
                        elif (c, s) == (3, 5):
                            exponentials(g, "a", 0)
                        elif (c, s) == (4, 1):
                            gate(g, G_A)
                        elif (c, s) == (4, 2):
                            act.wait_ge(conv_done, g + 1)
                            probs_out(g, "a", 8)
                        elif (c, s) == (5, 0):
                            evacuate(g, K_B, kbuf)
                        elif (c, s) == (5, 6):
                            keys_out(g, "b")
                        elif (c, s) == (6, 0):
                            evacuate(g, Q_B, qbuf)
                        elif (c, s) == (6, 3):
                            queries_out(g, "b")
                        elif (c, s) == (7, 0):
                            evacuate(g, V_B, vbuf)
                        elif (c, s) == (7, 4):
                            exponentials(g, "b", 1)
                        elif (c, s) == (7, 5):
                            exponentials(g, "b", 0)
                        elif (c, s) == (8, 1):
                            gate(g, G_B)
                        elif (c, s) == (8, 2):
                            probs_out(g, "b", 6)
                        elif (c, s) == (8, 5):
                            square_sums_b(g)
                        elif (c, s) == (9, 0):
                            evacuate(g, C_G, kbuf)
                        elif (c, s) == (10, 1):
                            shift_u(g)

            def x_squares(n):
                act.wait_ge(x_in[n], 16)
                if n > 0:
                    act.wait_ge(x_squared, n)
                for b in range(NB):
                    last = nc.scalar.activation(scratch2[:, b, :], resid[:, b, n * N:(n + 1) * N],
                                                ACT.Square, accum_out=ss_x[:, b, n:n + 1])
                last.then_inc(x_squared, 1)

            for i, v in enumerate((norm1_g, norm2_g)):
                act.dma_start(norm_rows[i * KT:(i + 1) * KT, :], v[0, :].rearrange("(k p) -> k p", p=P)) \
                    .then_inc(norm_in, 16)
            act.wait_ge(norm_turned, 1)
            nc.scalar.activation(norm_g[:, :, :].rearrange("p i k -> p (i k)"), acc[1][:, 0, 0:2 * KT],
                                 ACT.Copy).then_inc(norm_ready, 1)
            act.wait_ge(norm_ready, 1)
            act.wait_ge(first_turned, 1)
            high_scaled(0, 0, 0, (0, 1)).then_inc(first_hi, 1)
            round_weights(0, 0, reuse=False)
            act.wait_ge(side_full[0], 1)
            high_scaled(0, 0, 0, (2, 3)).then_inc(act_hi, 1)
            round_weights(0, 1, reuse=False)
            split_high_scaled(1, 1, 1, 0)
            round_weights(0, 2, reuse=False)
            group_chunks(0, [0])
            act.wait_ge(lam_sum, 1)
            nc.scalar.activation(lam_e[:, :], lam2[:, :], ACT.Exp).then_inc(lam_exp, 1)
            act.wait_ge(rx_done, 1)
            act.wait_ge(kq_gain_done, 2)
            group_chunks(0, [1])
            with act.Fori(0, GROUPS - 1) as i:
                group_chunks(i, range(2, NC))
                group_chunks(i + 1, range(2))
            group_chunks(GROUPS - 1, range(2, NC))

            def x1_squares(n):
                act.wait_ge(acc_read[n % 2], read_no(WO0 + n))
                if n > 0:
                    act.wait_ge(x1_squared, n)
                for b in range(NB):
                    last = nc.scalar.activation(scratch2[:, b, :], resid[:, b, n * N:(n + 1) * N],
                                                ACT.Square, accum_out=ss_h[:, b, n:n + 1])
                last.then_inc(x1_squared, 1)

            for n in range(GROUPS):
                for s in range(STEPS):
                    round_weights(WO0 + n, s + AHEAD)
                    if (n, s) == (0, 1):
                        gate(GROUPS - 1, G_C)
                    elif (n, s) == (0, 5):
                        split_high(0, side_no(0, GROUPS - 1, "mixT"), act_mid, GROUPS - 1)
                    elif n > 0 and s == 1:
                        x1_squares(n - 1)
                    elif n > 0 and s == 3:
                        split_high_scaled(0, H2_SIDE + n, n - 1, 1)

            def relu_out(f, j):
                result_of(f * MC + (MLP0 + j))
                for b in range(NB):
                    last = nc.scalar.activation(qbuf[:, b, :], acc[j % 2][:, b, :], ACT.Relu,
                                                scale=r_h[:, b:b + 1])
                last.then_inc(acc_read[j % 2], 1)

            def square_hidden(f, j):
                act.wait_ge(side_full[0], f * GROUPS + (HID_SIDE + j + 1))
                nc.scalar.activation(kbuf[:, :, :], side[0][:, :].rearrange("p (b n) -> p b n", b=NB),
                                     ACT.Square).then_inc(hid_squared, 1)

            def hidden_high(f, j):
                act.wait_ge(hid_squared, f * GROUPS + (j + 1))
                nc.scalar.activation(act_mid[:, 0, j * KT4:(j + 1) * KT4, :],
                                     kbuf[:, :, :].rearrange("p b (t k) -> p (b t) k", k=T),
                                     ACT.Copy).then_inc(act_hi, 1)

            def quarter_chunks(f, chunks, last_quarter=False):
                first = isinstance(f, int) and f == 0
                for j in chunks:
                    for s in range(STEPS):
                        if not (last_quarter and j == MC - 1 and s + AHEAD >= STEPS):
                            round_weights(f * MC + (MLP0 + j), s + AHEAD)
                        if first and j == 0:
                            if s == 1:
                                x1_squares(GROUPS - 1)
                            elif s == 3:
                                split_high_scaled(0, H2_SIDE + GROUPS, GROUPS - 1, 1)
                        if 1 <= j <= GROUPS:
                            if s == 0:
                                relu_out(f, j - 1)
                            elif s == 3:
                                square_hidden(f, j - 1)
                                hidden_high(f, j - 1)

            quarter_chunks(0, [0])
            act.wait_ge(rh_done, 1)
            with act.Fori(0, QUARTERS - 1) as i:
                quarter_chunks(i, range(1, MC))
                quarter_chunks(i + 1, [0])
            quarter_chunks(QUARTERS - 1, range(1, MC), last_quarter=True)

        @block.vector
        def _(dve):
            def low_weights(chunk, i, reuse=True):
                q, half = i % STEPS // 2, i % 2
                dve.wait_ge(hi_ready, chunk * STEPS + (i + 1))
                if reuse:
                    dve.wait_ge(step_done, chunk * STEPS + (i - RING + 1))
                nc.vector.tensor_tensor(w_lo[:, i % RING, :, :], raw[:, q, 2 * half:2 * half + 2, :],
                                        w_hi[:, i % RING, :, :].bitcast(F32), SUB).then_inc(lo_ready, 1)

            def result_of(chunk):
                dve.wait_ge(step_done, chunk * STEPS + STEPS)

            def mean_squares(g, e):
                dve.wait_ge(sq_done, g * 4 + (e + 1))
                nc.vector.tensor_reduce(sumsq[:, :], scratch.rearrange("p (i d) -> p i d", d=HD),
                                        AX.X, ADD).then_inc(ss_done, 1)
                dve.wait_ge(ss_done, g * 4 + (e + 1))
                nc.vector.tensor_scalar(meansq[:, :], sumsq[:, :], 1.0 / HD, EPS, MUL, ADD) \
                    .then_inc(ms_done, 1)

            def keys_low(g, br):
                i = "ab".index(br)
                dve.wait_ge(side_full[0], side_no(0, g, "kT_" + br))
                dve.wait_ge(k_hi, g * 2 + (i + 1))
                nc.vector.scalar_tensor_tensor(
                    out=kT[:, 1, :, :], in0=side[0][:, :].rearrange("p (m t) -> p m t", m=MAPS),
                    scalar=kq_gain[:, i:i + 1], in1=kT[:, 0, :, :].bitcast(F32), op0=MUL, op1=SUB) \
                    .then_inc(side_read[0], 1)

            def queries_low(g, br):
                dve.wait_ge(side_full[1], side_no(1, g, "qT_" + br))
                queries = side[1][:, :].rearrange("p (m t) -> p m t", m=MAPS)
                dve.wait_ge(q_hi, g * 2 + ("ab".index(br) + 1))
                nc.vector.tensor_copy(qT0[:, :, :], queries[:, :, 0:P])
                nc.vector.tensor_tensor(qT[:, 1, :, :], queries[:, :, P:T], qT[:, 0, :, :].bitcast(F32),
                                        SUB).then_inc(side_read[1], 1)

            def biased_scores(g, br, b):
                if b == 1:
                    dve.wait_ge(rstd_done, g * 4 + (2 if br == "a" else 4))
                    if br == "a":
                        dve.wait_ge(rel_ready, g + 1)
                pair, width = (0, T) if b == 1 else (1, P)
                dve.wait_ge(side_full[pair], side_no(pair, g, "scores_" + br))
                for m in range(MAPS):
                    if br == "a":
                        add = rel[:, m, width - 1::-1]
                    else:
                        add = mask[:, T - width:T]
                    o = s3[:, m, 0:T] if b == 1 else s3[:, m, T:T + P]
                    i = b * MAPS + m
                    last = nc.vector.scalar_tensor_tensor(
                        out=o, in0=side[pair][:, m * width:(m + 1) * width], scalar=r_q[:, i:i + 1],
                        in1=add, op0=MUL, op1=ADD)
                last.then_inc(side_read[pair], 1)

            def row_max(g, br):
                dve.wait_ge(side_read[1], side_no(1, g, "scores_" + br))
                nc.vector.tensor_reduce(neg_max[:, MAPS:2 * MAPS], s3[:, :, 0:T], AX.X, ALU.max,
                                        negate=True)
                nc.vector.tensor_reduce(neg_max[:, 0:MAPS], s3[:, :, T:T + P], AX.X, ALU.max,
                                        negate=True).then_inc(max_done, 1)

            def row_reciprocals(g, br):
                i = "ab".index(br)
                dve.wait_ge(exp_done, g * 2 + (i + 1))
                nc.vector.reciprocal(r_sum[:, :], row_sum[:, :]).then_inc(rsum_done, 1)

            def difference(g):
                dve.wait_ge(rsum_done, g * 2 + 2)
                pairs = row_sum[:, :].rearrange("p (i two) -> p i two", two=2)
                rpairs = r_sum[:, :].rearrange("p (i two) -> p i two", two=2)
                nc.vector.scalar_tensor_tensor(out=lam_ratio[:, :], in0=pairs[:, :, 0],
                                               scalar=neg_lam[:, 0:1], in1=rpairs[:, :, 1],
                                               op0=MUL, op1=MUL).then_inc(ratio_done, 1)
                dve.wait_ge(ratio_done, g + 1)
                for b in range(NB):
                    cols = slice(0, T) if b == 1 else slice(T, T + P)
                    for h in range(2):
                        i = 2 * b + h
                        last = nc.vector.scalar_tensor_tensor(
                            out=s3[:, 2 * h, cols], in0=s3[:, 2 * h + 1, cols],
                            scalar=lam_ratio[:, i:i + 1], in1=s3[:, 2 * h, cols], op0=MUL, op1=ADD)
                last.then_inc(comb_done, 1)

            def gate_sum(g, c, j):
                result_of(chunk_of(g, c))
                dve.wait_ge(gateb_in, g * 16 + 16)
                for b in range(NB):
                    last = nc.vector.scalar_tensor_tensor(
                        out=gbuf[:, b, :], in0=acc[c % 2][:, b, :], scalar=r_x[:, b:b + 1],
                        in1=gate_b[:, j, :], op0=MUL, op1=ADD)
                last.then_inc(acc_read[c % 2], 1)

            def probs_out_a(g):
                dve.wait_ge(side_full[1], side_no(1, g, "pT_a"))
                nc.vector.tensor_copy(pT[:, 8:12, :], side[1][:, 0:N].rearrange("p (t k) -> p t k", k=P)) \
                    .then_inc(side_read[1], 1)

            def out_a(g, b):
                if b == 0:
                    dve.wait_ge(side_full[1], side_no(1, g, "out_a"))
                    dve.wait_ge(gate_done, g * 3 + 1)
                    dve.wait_ge(rsum_done, g * 2 + 1)
                for m in range(MAPS):
                    cols = slice(m * HD, (m + 1) * HD)
                    i = b * MAPS + m
                    last = nc.vector.scalar_tensor_tensor(
                        out=mix[:, b, cols], in0=side[1][:, b * N + m * HD:b * N + (m + 1) * HD],
                        scalar=r_sum[:, i:i + 1], in1=gbuf[:, b, cols], op0=MUL, op1=MUL)
                if b == 1:
                    last.then_inc(side_read[1], 1)

            def mean_squares_b(g):
                dve.wait_ge(ssb_done, g + 1)
                nc.vector.tensor_scalar(ms_b[:, :], ss_b[:, :], 1.0 / (2 * HD), EPS, MUL, ADD) \
                    .then_inc(msb_done, 1)

            def out_b(g):
                dve.wait_ge(rstdb_done, g + 1)
                first_sums = r_sum[:, :].rearrange("p (i two) -> p i two", two=2)[:, :, 0]
                nc.vector.tensor_tensor(coef_b[:, :], first_sums, r_b[:, :], MUL).then_inc(coefb_done, 1)
                dve.wait_ge(coefb_done, g + 1)
                for b in range(NB):
                    for h in range(2):
                        i = 2 * b + h
                        cols = slice(b * N + h * 2 * HD, b * N + (h + 1) * 2 * HD)
                        last = nc.vector.scalar_tensor_tensor(
                            out=scratch[:, cols], in0=side[1][:, cols], scalar=coef_b[:, i:i + 1],
                            in1=sub_g[:, h, :], op0=MUL, op1=MUL)
                last.then_inc(side_read[1], 1)

            def times(g, c, dst):
                result_of(chunk_of(g, c))
                for b in range(NB):
                    last = nc.vector.scalar_tensor_tensor(
                        out=dst[:, b, :], in0=acc[c % 2][:, b, :], scalar=r_x[:, b:b + 1],
                        in1=dst[:, b, :], op0=MUL, op1=MUL)
                last.then_inc(acc_read[c % 2], 1)

            def add_c(g):
                dve.wait_ge(gate_done, g * 3 + 3)
                dve.wait_ge(acc_read[B_G % 2], acc_no(g, NC, B_G))
                nc.vector.tensor_tensor(kbuf[:, :, :], kbuf[:, :, :], gbuf[:, :, :], MUL) \
                    .then_inc(gated_c, 1)
                dve.wait_ge(gated_c, g + 1)
                dve.wait_ge(mixb_done, g + 1)
                nc.vector.tensor_tensor(mix[:, :, :], mix[:, :, :], kbuf[:, :, :], ADD) \
                    .then_inc(mix_done, 1)

            def low_scaled(pair, n, norm, tiles=range(KT4)):
                for t in tiles:
                    k = n * KT4 + t
                    last = nc.vector.scalar_tensor_tensor(
                        out=act_in[:, 1, k, :], in0=side[pair][:, t * T:(t + 1) * T],
                        scalar=norm_g[:, norm, k:k + 1], in1=act_in[:, 0, k, :].bitcast(F32),
                        op0=MUL, op1=SUB)
                return last

            def split_low_scaled(pair, no, hi_no, n, norm):
                dve.wait_ge(side_full[pair], no)
                dve.wait_ge(act_hi, hi_no)
                low_scaled(pair, n, norm).then_inc(side_read[pair], 1)

            def split_low(pair, no, hi_no, dst, n):
                dve.wait_ge(side_full[pair], no)
                dve.wait_ge(act_hi, hi_no)
                tiles = bass.ds(n * KT4, KT4)
                nc.vector.tensor_tensor(dst[:, 1, tiles, :],
                                        side[pair][:, :].rearrange("p (t k) -> p t k", t=KT4),
                                        dst[:, 0, tiles, :].bitcast(F32), SUB).then_inc(side_read[pair], 1)

            def group_chunks(g, chunks):
                first = isinstance(g, int) and g == 0
                for c in chunks:
                    for s in range(STEPS):
                        low_weights(chunk_of(g, c), s + AHEAD, reuse=not (first and c == 0 and s == 0))
                        if c == 0 and first:
                            if s == 2:
                                split_low_scaled(0, 2, 3, 2, 0)
                            elif s == 3:
                                extend_rel_rows()
                            elif s == 4:
                                split_low_scaled(1, 2, 4, 3, 0)
                            elif s == 5:
                                prepare_gains()
                            elif s == 6:
                                lambda_products()
                            elif s == 7:
                                mean_squares_x()
                        if first and (c, s) == (1, 0):
                            negative_lambda()
                            dve.wait_ge(rx_done, 1)
                        if c == 0 and not first:
                            if s == 0:
                                dve.wait_ge(mixb_done, g)
                                gate_sum(g - 1, G_C, 2)
                            elif s == 3:
                                add_c(g - 1)
                            elif s == 6:
                                split_low(0, side_no(0, g - 1, "mixT"), g + GROUPS, act_mid, g - 1)
                        if (c, s) == (1, 2):
                            mean_squares(g, 0)
                        elif (c, s) == (1, 6):
                            keys_low(g, "a")
                        elif (c, s) == (2, 2):
                            mean_squares(g, 1)
                        elif (c, s) == (2, 3):
                            queries_low(g, "a")
                        elif (c, s) == (3, 1):
                            biased_scores(g, "a", 1)
                        elif (c, s) == (3, 2):
                            biased_scores(g, "a", 0)
                        elif (c, s) == (3, 3):
                            row_max(g, "a")
                        elif (c, s) == (3, 7):
                            row_reciprocals(g, "a")
                        elif (c, s) == (4, 0):
                            gate_sum(g, G_A, 0)
                        elif (c, s) == (4, 2):
                            dve.wait_ge(conv_done, g + 1)
                            probs_out_a(g)
                        elif (c, s) == (4, 6):
                            out_a(g, 0)
                        elif (c, s) == (4, 7):
                            out_a(g, 1)
                        elif (c, s) == (5, 2):
                            mean_squares(g, 2)
                        elif (c, s) == (5, 6):
                            keys_low(g, "b")
                        elif (c, s) == (6, 2):
                            mean_squares(g, 3)
                        elif (c, s) == (6, 3):
                            queries_low(g, "b")
                        elif (c, s) == (7, 1):
                            biased_scores(g, "b", 1)
                        elif (c, s) == (7, 2):
                            biased_scores(g, "b", 0)
                        elif (c, s) == (7, 3):
                            row_max(g, "b")
                        elif (c, s) == (7, 7):
                            row_reciprocals(g, "b")
                            difference(g)
                        elif (c, s) == (8, 0):
                            gate_sum(g, G_B, 1)
                        elif (c, s) == (8, 6):
                            mean_squares_b(g)
                        elif (c, s) == (9, 0):
                            out_b(g)
                        elif (c, s) == (10, 0):
                            dve.wait_ge(acc_read[C_G % 2], acc_no(g, NC, C_G))
                            times(g, X_C, kbuf)
                        elif (c, s) == (11, 0):
                            dve.wait_ge(conv_done, g + 2)
                            times(g, B_G, kbuf)

            def mean_squares_x():
                dve.wait_ge(x_squared, GROUPS)
                nc.vector.tensor_reduce(ms_x[:, :], ss_x[:, :, :], AX.X, ADD).then_inc(ssx_done, 1)
                dve.wait_ge(ssx_done, 1)
                nc.vector.tensor_scalar(ms_x[:, :], ms_x[:, :], 1.0 / D, EPS, MUL, ADD).then_inc(msx_done, 1)

            def extend_rel_rows():
                dve.wait_ge(rel_in, 16)
                nc.vector.tensor_copy(rel_rows[:, REL:EXT],
                                      rel_rows[:, REL - 1:REL].to_broadcast([D // HD, EXT - REL])) \
                    .then_inc(rel_rows_done, 1)

            def prepare_gains():
                dve.wait_ge(small_in, 16 * 10)
                for i in range(2):
                    nc.vector.scalar_tensor_tensor(out=kq_gain[:, i:i + 1], in0=gains[:, 2 * i:2 * i + 1],
                                                   scalar=SCALE, in1=gains[:, 2 * i + 1:2 * i + 2],
                                                   op0=MUL, op1=MUL).then_inc(kq_gain_done, 1)
                nc.vector.tensor_scalar(sub_g[:, :, :], sub_g[:, :, :], 1.0 - LAMBDA_INIT, None, MUL) \
                    .then_inc(conv_done, 1)

            def lambda_products():
                for i in range(2):
                    nc.vector.tensor_tensor(lam_v[:, 2 * i, :], lam_v[:, 2 * i, :], lam_v[:, 2 * i + 1, :],
                                            MUL).then_inc(lam_prod, 1)
                dve.wait_ge(lam_prod, 2)
                nc.vector.tensor_reduce(lam2[:, :], lam_v[:, 0:4:2, :], AX.X, ADD).then_inc(lam_sum, 1)

            def negative_lambda():
                dve.wait_ge(lam_exp, 1)
                nc.vector.tensor_tensor(neg_lam[:, :], lam_e[:, 1:2], lam_e[:, 0:1], SUB) \
                    .then_inc(lam_diff, 1)
                dve.wait_ge(lam_diff, 1)
                nc.vector.tensor_scalar(neg_lam[:, :], neg_lam[:, :], LAMBDA_INIT, None, SUB) \
                    .then_inc(lam_done, 1)

            dve.wait_ge(norm_ready, 1)
            dve.wait_ge(first_hi, 1)
            low_scaled(0, 0, 0, (0, 1)).then_inc(first_lo, 1)
            low_weights(0, 0, reuse=False)
            dve.wait_ge(act_hi, 1)
            low_scaled(0, 0, 0, (2, 3)).then_inc(side_read[0], 1)
            low_weights(0, 1, reuse=False)
            split_low_scaled(1, 1, 2, 1, 0)
            low_weights(0, 2, reuse=False)
            group_chunks(0, range(2))
            dve.wait_ge(lam_done, 1)
            dve.wait_ge(conv_done, 1)
            dve.wait_ge(mask_ready, 1)
            with dve.Fori(0, GROUPS - 1) as i:
                group_chunks(i, range(2, NC))
                group_chunks(i + 1, range(2))
            group_chunks(GROUPS - 1, range(2, NC))

            def add_residual(chunk, parity, n):
                result_of(chunk)
                cols = slice(n * N, (n + 1) * N)
                nc.vector.tensor_tensor(resid[:, :, cols], acc[parity][:, :, :], resid[:, :, cols], ADD) \
                    .then_inc(acc_read[parity], 1)

            HI0 = 2 * GROUPS
            for n in range(GROUPS):
                for s in range(STEPS):
                    low_weights(WO0 + n, s + AHEAD)
                    if n == 0:
                        if s == 0:
                            dve.wait_ge(mixb_done, GROUPS)
                            gate_sum(GROUPS - 1, G_C, 2)
                        elif s == 3:
                            add_c(GROUPS - 1)
                        elif s == 5:
                            split_low(0, side_no(0, GROUPS - 1, "mixT"), HI0, act_mid, GROUPS - 1)
                    elif s == 0:
                        add_residual(WO0 + n - 1, (n - 1) % 2, n - 1)
                    elif s == 4:
                        split_low_scaled(0, H2_SIDE + n, HI0 + n, n - 1, 1)

            def quarter_chunks(f, chunks, last_quarter=False):
                first = isinstance(f, int) and f == 0
                for j in chunks:
                    for s in range(STEPS):
                        if not (last_quarter and j == MC - 1 and s + AHEAD >= STEPS):
                            low_weights(f * MC + (MLP0 + j), s + AHEAD)
                        if first and j == 0:
                            if s == 0:
                                add_residual(MLP0 - 1, 1, GROUPS - 1)
                            elif s == 3:
                                dve.wait_ge(x1_squared, GROUPS)
                                nc.vector.tensor_reduce(ms_h[:, :], ss_h[:, :, :], AX.X, ADD) \
                                    .then_inc(ssh_done, 1)
                                dve.wait_ge(ssh_done, 1)
                                nc.vector.tensor_scalar(ms_h[:, :], ms_h[:, :], 1.0 / D, EPS, MUL, ADD) \
                                    .then_inc(msh_done, 1)
                            elif s == 4:
                                split_low_scaled(0, H2_SIDE + GROUPS, HI0 + GROUPS, GROUPS - 1, 1)
                        elif j == 0 and s == 0:
                            add_residual(f * MC + (MLP0 - 1), 1, GROUPS - 1)
                        if 1 <= j <= GROUPS and s == 4:
                            dve.wait_ge(act_hi, f * GROUPS + (HI0 + GROUPS + j))
                            tiles = slice((j - 1) * KT4, j * KT4)
                            nc.vector.tensor_tensor(
                                act_mid[:, 1, tiles, :],
                                kbuf[:, :, :].rearrange("p b (t k) -> p (b t) k", k=T),
                                act_mid[:, 0, tiles, :].bitcast(F32), SUB).then_inc(side_read[0], 1)
                        if j > GROUPS and s == 0:
                            add_residual(f * MC + (MLP0 + j - 1), (j - 1) % 2, j - 1 - GROUPS)

            quarter_chunks(0, [0])
            with dve.Fori(0, QUARTERS - 1) as i:
                quarter_chunks(i, range(1, MC))
                quarter_chunks(i + 1, [0])
            quarter_chunks(QUARTERS - 1, range(1, MC), last_quarter=True)
            for b in range(NB):
                if b == 0:
                    dve.wait_ge(block_done, 1)
                else:
                    result_of(MLP0 + QUARTERS * MC - 1)
                nc.vector.tensor_tensor(resid[:, b, D - N:D], acc[1][:, b, :], resid[:, b, D - N:D], ADD) \
                    .then_inc(block_summed, 1)

        @block.gpsimd
        def _(pool):
            nc.gpsimd.memset(ident[:, :], 0.0).then_inc(ident_set, 1)
            nc.gpsimd.memset(mask[:, :], 0.0).then_inc(mask_set, 1)
            pool.wait_ge(ident_set, 1)
            nc.gpsimd.affine_select(out=ident[:, :], in_=ident[:, :], compare_op=ALU.not_equal, fill=1.0,
                                    base=0, pattern=[[-1, P]], channel_multiplier=1) \
                .then_inc(ident_ready, 1)
            pool.wait_ge(mask_set, 1)
            nc.gpsimd.memset(mask[0:CHUNK, T - CHUNK:T], NEG).then_inc(mask_ready, 1)
            nc.gpsimd.memset(neg_half[:, :], -0.5).then_inc(half_ready, 1)
            pool.wait_ge(half_ready, 1)

            def rsqrt(dst, src, n):
                return nc.gpsimd.tensor_tensor(dst, src, neg_half[:, 0:n], ALU.pow)

            pool.dma_start(rel_rows[:, 0:REL], a_rel_bias[0]).then_inc(rel_in, 16)
            for i, v in enumerate((a_qn_g, a_kn_g, b_qn_g, b_kn_g)):
                pool.dma_start(gains[:, i:i + 1], v[0, :].rearrange("(d o) -> d o", o=1)) \
                    .then_inc(small_in, 16)
            for i, v in enumerate((b_lq1, b_lk1, b_lq2, b_lk2)):
                pool.dma_start(lam_v[:, i, :], v[0, :].partition_broadcast(P)).then_inc(small_in, 16)
            for i in range(2):
                pool.dma_start(sub_g[:, i, :], b_subln_g[0, :].partition_broadcast(P)) \
                    .then_inc(small_in, 16)
            pool.wait_ge(rel_rows_done, 1)
            pool.dma_start(rel_ext.ap(), rel_rows[:, :]).then_inc(rel_stored, 16)
            pool.wait_ge(msx_done, 1)
            rsqrt(r_x[:, :], ms_x[:, :], NB).then_inc(rx_done, 1)

            def square(g, c, src, e):
                pool.wait_ge(acc_read[c % 2], acc_no(g, NC, c))
                nc.gpsimd.tensor_tensor(scratch2, src[:, :, :], src[:, :, :], MUL).then_inc(sq_done, 1)

            def rms(g, dst, e):
                pool.wait_ge(ms_done, g * 4 + (e + 1))
                rsqrt(dst[:, :], meansq[:, :], 8).then_inc(rstd_done, 1)

            def normalise_keys(g, e, i):
                pool.wait_ge(rstd_done, g * 4 + (e + 1))
                k3 = kbuf[:, :, :].rearrange("p b (m d) -> p (b m) d", d=HD)
                nc.gpsimd.tensor_tensor(k3, k3, r_k[:, :].unsqueeze(2).to_broadcast([P, 8, HD]), MUL) \
                    .then_inc(kn_done, 1)

            def mask_bias(g):
                pool.wait_ge(rel_loaded, g * 16 + 16)
                masked = rel[0:CHUNK, :, 0:CHUNK]
                neg = mask[0:CHUNK, T - CHUNK:T].unsqueeze(1).to_broadcast([CHUNK, MAPS, CHUNK])
                nc.gpsimd.tensor_tensor(masked, masked, neg, ADD).then_inc(rel_ready, 1)

            def add_b(g):
                pool.wait_ge(side_read[1], side_no(1, g, "out_b"))
                pool.wait_ge(gate_done, g * 3 + 2)
                nc.gpsimd.tensor_tensor(scratch2, scratch2, gbuf[:, :, :], MUL).then_inc(outb_gated, 1)
                pool.wait_ge(outb_gated, g + 1)
                nc.gpsimd.tensor_tensor(mix[:, :, :], mix[:, :, :], scratch2, ADD).then_inc(mixb_done, 1)

            def convolve(g):
                pool.wait_ge(shifted, g * 64 + 64)
                pool.wait_ge(taps_in, g * 16 + 16)
                for tap, t in ((0, u2), (1, u1), (2, kbuf)):
                    for b in range(NB):
                        nc.gpsimd.tensor_tensor(t[:, b, :], t[:, b, :], conv_w[:, tap, :], MUL) \
                            .then_inc(taps_done, 1)
                pool.wait_ge(taps_done, g * 6 + 6)
                nc.gpsimd.tensor_tensor(u1, u1, u2, ADD).then_inc(tap_sum, 1)
                pool.wait_ge(tap_sum, g + 1)
                nc.gpsimd.tensor_tensor(kbuf[:, :, :], kbuf[:, :, :], u1, ADD).then_inc(conv_done, 1)

            def group(g):
                square(g, K_A, kbuf, 0)
                rms(g, r_k, 0)
                normalise_keys(g, 0, 0)
                mask_bias(g)
                square(g, Q_A, qbuf, 1)
                rms(g, r_q, 1)
                square(g, K_B, kbuf, 2)
                rms(g, r_k, 2)
                normalise_keys(g, 2, 1)
                square(g, Q_B, qbuf, 3)
                rms(g, r_q, 3)
                pool.wait_ge(ssb_done, g + 1)
                pool.wait_ge(msb_done, g + 1)
                rsqrt(r_b[:, :], ms_b[:, :], 4).then_inc(rstdb_done, 1)
                nc.gpsimd.memset(pbuf[0:2, 0:N], 0.0)
                nc.gpsimd.memset(pbuf[0:2, NB * N:NB * N + N], 0.0).then_inc(zero_rows, 1)
                add_b(g)
                convolve(g)

            with pool.Fori(0, GROUPS) as g:
                group(g)
            pool.wait_ge(msh_done, 1)
            rsqrt(r_h[:, :], ms_h[:, :], NB).then_inc(rh_done, 1)


_INS = ["x", "norm1_g", "w_in", "w_gate", "b_gate", "a_qn_g", "a_kn_g", "a_rel_bias", "b_qn_g", "b_kn_g",
        "b_lq1", "b_lk1", "b_lq2", "b_lk2", "b_subln_g", "c_conv_w", "w_o", "norm2_g", "w_mlp1", "w_mlp2"]


def kernel(**inputs):
    import numpy as _np
    import concourse.bacc as _bacc
    from concourse import mybir as _mybir
    from concourse.bass_utils import run_bass_kernel_spmd as _run

    nc = _bacc.Bacc("TRN2", target_bir_lowering=False, num_devices=1)
    arrays, args = {}, []
    for name in _INS:
        a = _np.ascontiguousarray(inputs[name])
        arrays[f"in_{name}_dram"] = a
        args.append(nc.dram_tensor(f"in_{name}_dram", a.shape, _mybir.dt.from_np(a.dtype),
                                   kind="ExternalInput").ap())
    shape = arrays["in_x_dram"].shape
    args.append(nc.dram_tensor("out_dram", shape, _mybir.dt.float32, kind="ExternalOutput").ap())
    build_trunk(nc, *args)
    r = _run(nc, [arrays], core_ids=[0])
    return r.results[0]["out_dram"]
```
